# Optimizing a Trainium2 kernel written in Bass

```python
import math
import jax, jax.numpy as jnp
from jax import lax
import numpy as np

D_MODEL = 1024
BATCH = 1
SEQ = 512
DEPTH = 2
DEC_BATCH = 8
DEC_SEQ = 1
PAST_LEN = 512
PAGE_SIZE = 128

N_MIXERS = 2
N_HEADS = 16
HEAD_DIM = D_MODEL // N_HEADS
D_FF = 2816
CONV_WIDTH = 31
D_PLE = 256
Q_BLOCK = 128
RMS_EPS = 1e-6
LN_EPS = 1e-5
LOGIT_BIAS_INIT = -7.0
N_ATTN_LAYERS = (DEPTH + 1) // 2
N_CONV_LAYERS = DEPTH // 2

kernel_name = "stickbreaking_conformer_macaron_step"

def rmsnorm(x, g):
    xf = x.astype(jnp.float32)
    y = xf * lax.rsqrt(jnp.mean(xf * xf, axis=-1, keepdims=True) + RMS_EPS) * g.astype(jnp.float32)
    return y.astype(x.dtype)

def layernorm(x, g, b):
    xf = x.astype(jnp.float32)
    mu = jnp.mean(xf, axis=-1, keepdims=True)
    var = jnp.mean(jnp.square(xf - mu), axis=-1, keepdims=True)
    y = (xf - mu) * lax.rsqrt(var + LN_EPS) * g.astype(jnp.float32) + b.astype(jnp.float32)
    return y.astype(x.dtype)

def swiglu(h, wg, wu, wd):
    return (jax.nn.silu(h @ wg) * (h @ wu)) @ wd

def qkv_project(h, w_qkv, q_gain, k_gain):
    B, T, _ = h.shape
    qkv = (h @ w_qkv).reshape(B, T, 3, N_HEADS, HEAD_DIM)
    q = rmsnorm(qkv[:, :, 0], q_gain)
    k = rmsnorm(qkv[:, :, 1], k_gain)
    return q, k, qkv[:, :, 2]

def sb_attend(q, k, v, bias, q_pos, k_pos):
    scale = 1.0 / math.sqrt(q.shape[-1])
    z = jnp.einsum('bqhd,bkhd->bhqk', q, k).astype(jnp.float32) * scale \
        + bias.astype(jnp.float32)[None, :, None, None]
    mask = k_pos[None, :] < q_pos[:, None]
    log_not = jnp.where(mask, jax.nn.log_sigmoid(-z), 0.0)
    after = lax.cumsum(log_not, axis=3, reverse=True) - log_not
    a = jnp.where(mask, jnp.exp(jax.nn.log_sigmoid(z) + after), 0.0)
    return jnp.einsum('bhqk,bkhd->bqhd', a.astype(v.dtype), v)

def sb_prompt(q, k, v, bias):
    B, T, H, Dh = q.shape
    nb = T // Q_BLOCK
    qb = q.reshape(B, nb, Q_BLOCK, H, Dh).transpose(1, 0, 2, 3, 4)
    pos = jnp.arange(T, dtype=jnp.int32)
    posb = pos.reshape(nb, Q_BLOCK)
    ob = lax.map(lambda a: sb_attend(a[0], k, v, bias, a[1], pos), (qb, posb))
    return ob.transpose(1, 0, 2, 3, 4).reshape(B, T, H, Dh)

def conv_module(h, buf, w_in, w_dw, b_dw, ln_g, ln_b, w_out):
    u = h @ w_in
    g = u[..., :D_MODEL] * jax.nn.sigmoid(u[..., D_MODEL:])
    xc = jnp.concatenate([buf.astype(g.dtype), g], axis=1)
    y = lax.conv_general_dilated(xc, w_dw[:, None, :].astype(xc.dtype), window_strides=(1,),
                                 padding='VALID', dimension_numbers=('NWC', 'WIO', 'NWC'),
                                 feature_group_count=D_MODEL) + b_dw
    y = jax.nn.silu(layernorm(y, ln_g, ln_b))
    return y @ w_out, xc[:, -(CONV_WIDTH - 1):]

def setup_inputs(seed: int = 0) -> dict:
    key = jax.random.key(seed)
    ks = iter(jax.random.split(key, 48))
    f32 = jnp.float32

    def nrm(shape, scale):
        return jax.random.normal(next(ks), shape, f32) * scale

    def gain(shape):
        return 1.0 + 0.05 * jax.random.normal(next(ks), shape, f32)

    n_pages = PAST_LEN // PAGE_SIZE
    n_used = DEC_BATCH * n_pages
    n_phys = n_used + max(1, n_used // 4)
    page_table = jax.random.permutation(next(ks), n_phys)[:n_used].reshape(DEC_BATCH, n_pages).astype(jnp.int32)

    return {
        "x_prompt": nrm((BATCH, SEQ, D_MODEL), 1.0),
        "x_sample": nrm((DEC_BATCH, DEC_SEQ, D_MODEL), 1.0),
        "cache_k": nrm((N_ATTN_LAYERS, n_phys, PAGE_SIZE, N_HEADS, HEAD_DIM), 1.0),
        "cache_v": nrm((N_ATTN_LAYERS, n_phys, PAGE_SIZE, N_HEADS, HEAD_DIM), 1.0),
        "state_conv": nrm((N_CONV_LAYERS, DEC_BATCH, CONV_WIDTH - 1, D_MODEL), 0.5),
        "page_table": page_table,
        "p_prompt": nrm((DEPTH, BATCH, SEQ, D_PLE), 1.0),
        "p_sample": nrm((DEPTH, DEC_BATCH, DEC_SEQ, D_PLE), 1.0),
        "norm_ffn1": gain((DEPTH, D_MODEL)),
        "ffn1_wg": nrm((DEPTH, D_MODEL, D_FF), D_MODEL ** -0.5),
        "ffn1_wu": nrm((DEPTH, D_MODEL, D_FF), D_MODEL ** -0.5),
        "ffn1_wd": nrm((DEPTH, D_FF, D_MODEL), D_FF ** -0.5),
        "norm_mix": gain((DEPTH, D_MODEL)),
        "attn_w_qkv": nrm((N_ATTN_LAYERS, D_MODEL, 3 * D_MODEL), D_MODEL ** -0.5),
        "attn_q_norm": gain((N_ATTN_LAYERS, HEAD_DIM)),
        "attn_k_norm": gain((N_ATTN_LAYERS, HEAD_DIM)),
        "attn_logit_bias": LOGIT_BIAS_INIT + nrm((N_ATTN_LAYERS, N_HEADS), 0.1),
        "attn_w_o": nrm((N_ATTN_LAYERS, D_MODEL, D_MODEL), D_MODEL ** -0.5),
        "conv_w_in": nrm((N_CONV_LAYERS, D_MODEL, 2 * D_MODEL), D_MODEL ** -0.5),
        "conv_w_dw": nrm((N_CONV_LAYERS, CONV_WIDTH, D_MODEL), CONV_WIDTH ** -0.5),
        "conv_b_dw": nrm((N_CONV_LAYERS, D_MODEL), 0.02),
        "conv_ln_g": gain((N_CONV_LAYERS, D_MODEL)),
        "conv_ln_b": nrm((N_CONV_LAYERS, D_MODEL), 0.02),
        "conv_w_out": nrm((N_CONV_LAYERS, D_MODEL, D_MODEL), D_MODEL ** -0.5),
        "norm_ffn2": gain((DEPTH, D_MODEL)),
        "ffn2_wg": nrm((DEPTH, D_MODEL, D_FF), D_MODEL ** -0.5),
        "ffn2_wu": nrm((DEPTH, D_MODEL, D_FF), D_MODEL ** -0.5),
        "ffn2_wd": nrm((DEPTH, D_FF, D_MODEL), D_FF ** -0.5),
        "norm_ple": gain((DEPTH, D_MODEL)),
        "ple_w_gate": nrm((DEPTH, D_MODEL, D_MODEL), D_MODEL ** -0.5),
        "ple_w_proj": nrm((DEPTH, D_PLE, D_MODEL), D_PLE ** -0.5),
    }

def reference(x_prompt, x_sample, cache_k, cache_v, state_conv, page_table, p_prompt, p_sample,
              norm_ffn1, ffn1_wg, ffn1_wu, ffn1_wd, norm_mix,
              attn_w_qkv, attn_q_norm, attn_k_norm, attn_logit_bias, attn_w_o,
              conv_w_in, conv_w_dw, conv_b_dw, conv_ln_g, conv_ln_b, conv_w_out,
              norm_ffn2, ffn2_wg, ffn2_wu, ffn2_wd, norm_ple, ple_w_gate, ple_w_proj):
    xp, xs = x_prompt, x_sample
    Bp, Tp, _ = xp.shape
    Bs, Ts, _ = xs.shape
    kp_l, vp_l, ks_l, vs_l, cp_l, cs_l = [], [], [], [], [], []
    for i in range(DEPTH):
        xp = xp + 0.5 * swiglu(rmsnorm(xp, norm_ffn1[i]), ffn1_wg[i], ffn1_wu[i], ffn1_wd[i])
        xs = xs + 0.5 * swiglu(rmsnorm(xs, norm_ffn1[i]), ffn1_wg[i], ffn1_wu[i], ffn1_wd[i])
        hp = rmsnorm(xp, norm_mix[i])
        hs = rmsnorm(xs, norm_mix[i])
        j = i // N_MIXERS
        if i % N_MIXERS == 0:
            bias = attn_logit_bias[j]
            qp, kp, vp = qkv_project(hp, attn_w_qkv[j], attn_q_norm[j], attn_k_norm[j])
            op = sb_prompt(qp, kp, vp, bias)
            qs, ks_, vs = qkv_project(hs, attn_w_qkv[j], attn_q_norm[j], attn_k_norm[j])
            past_k = cache_k[j][page_table].reshape(Bs, -1, N_HEADS, HEAD_DIM).astype(ks_.dtype)
            past_v = cache_v[j][page_table].reshape(Bs, -1, N_HEADS, HEAD_DIM).astype(vs.dtype)
            past = past_k.shape[1]
            k_all = jnp.concatenate([past_k, ks_], axis=1)
            v_all = jnp.concatenate([past_v, vs], axis=1)
            q_pos = past + jnp.arange(Ts, dtype=jnp.int32)
            k_pos = jnp.arange(past + Ts, dtype=jnp.int32)
            os_ = sb_attend(qs, k_all, v_all, bias, q_pos, k_pos)
            xp = xp + op.reshape(Bp, Tp, D_MODEL) @ attn_w_o[j]
            xs = xs + os_.reshape(Bs, Ts, D_MODEL) @ attn_w_o[j]
            kp_l.append(kp); vp_l.append(vp); ks_l.append(ks_); vs_l.append(vs)
        else:
            zero_buf = jnp.zeros((Bp, CONV_WIDTH - 1, D_MODEL), hp.dtype)
            mp, bufp = conv_module(hp, zero_buf, conv_w_in[j], conv_w_dw[j], conv_b_dw[j],
                                   conv_ln_g[j], conv_ln_b[j], conv_w_out[j])
            ms, bufs = conv_module(hs, state_conv[j], conv_w_in[j], conv_w_dw[j], conv_b_dw[j],
                                   conv_ln_g[j], conv_ln_b[j], conv_w_out[j])
            xp = xp + mp
            xs = xs + ms
            cp_l.append(bufp); cs_l.append(bufs)
        xp = xp + 0.5 * swiglu(rmsnorm(xp, norm_ffn2[i]), ffn2_wg[i], ffn2_wu[i], ffn2_wd[i])
        xs = xs + 0.5 * swiglu(rmsnorm(xs, norm_ffn2[i]), ffn2_wg[i], ffn2_wu[i], ffn2_wd[i])
        xp = xp + jax.nn.sigmoid(rmsnorm(xp, norm_ple[i]) @ ple_w_gate[i]) * (p_prompt[i].astype(xp.dtype) @ ple_w_proj[i])
        xs = xs + jax.nn.sigmoid(rmsnorm(xs, norm_ple[i]) @ ple_w_gate[i]) * (p_sample[i].astype(xs.dtype) @ ple_w_proj[i])
    new_k_prompt = jnp.stack(kp_l)
    new_v_prompt = jnp.stack(vp_l)
    new_k_sample = jnp.stack(ks_l)
    new_v_sample = jnp.stack(vs_l)
    new_conv_prompt = jnp.stack(cp_l)
    new_conv_sample = jnp.stack(cs_l)
    return (xp, xs, new_k_prompt, new_v_prompt, new_k_sample, new_v_sample, new_conv_prompt, new_conv_sample)


_drawn_inputs = setup_inputs


def setup_inputs(seed=0):
    import zlib

    import numpy as np

    out = dict(_drawn_inputs(seed))
    spreads = {}
    factors = {'attn_q_norm': 64.0,
     'attn_logit_bias': 64.0,
     'conv_b_dw': 3.374,
     'conv_ln_b': 6.621,
     'norm_ple': 4.886,
     'cache_v': 8.0,
     'attn_w_o': 8.0}
    for name, (base, spread) in spreads.items():
        noise = np.random.default_rng([zlib.crc32(name.encode()), seed]).standard_normal(out[name].shape)
        drawn = base * np.exp(spread * noise) if base else spread * noise
        out[name] = __import__('jax').numpy.asarray(drawn.astype(out[name].dtype))
    for name, factor in factors.items():
        out[name] = (out[name] * factor).astype(out[name].dtype)
    return out
```

```python
from contextlib import ExitStack

import concourse.bass as bass
from concourse import mybir

F32 = mybir.dt.float32
F32R = mybir.dt.float32r
I32 = mybir.dt.int32
ACT = mybir.ActivationFunctionType
ALU = mybir.AluOpType
AX = mybir.AxisListType
ds = bass.ds

P = 128
D = 1024
KD = D // P
FF = 2816
KF = FF // P
KH = KF // 2
TP = 512
NT = TP // P
NS = 8
T = TP + NS
HALF = T // 2
NH = 16
HD = 64
NP = KD
PG = 4
TAPS = 31
PAD = TAPS - 1
TAPS_DVE = 13
TAPS_ACT = TAPS - TAPS_DVE
RING = 4
DP = 256
KP = DP // P
EPS = 1e-6
LN_EPS = 1e-5
SLAB = KH * P
LOG_EXP = "natural_log_exp_and_others"
NORMS = ("norm_ffn1", "norm_mix", "norm_ffn2", "norm_ple")
VECS = 11 * KD


def build(nc, io):
    ctx = ExitStack()
    with ctx:
        def sb(name, shape, dt=F32):
            return ctx.enter_context(nc.sbuf_tensor(name, shape, dt))

        def sem(name):
            return ctx.enter_context(nc.semaphore(name))

        x = sb("x", [P, KD, T])
        h_hi = sb("h_hi", [P, KD, T], F32R)
        h_lo = sb("h_lo", [P, KD, T], F32R)
        w_raw = sb("w_raw", [P, 2, SLAB])
        w_hi = sb("w_hi", [P, 2, SLAB], F32R)
        w_lo = sb("w_lo", [P, 2, SLAB], F32R)
        square = sb("square", [P, 2, T])
        sumsq = sb("sumsq", [P, T])
        log_ms = sb("log_ms", [P, T])
        rms = sb("rms", [P, T])
        s_gate = sb("s_gate", [P, T])
        s_up = sb("s_up", [P, T])
        s_act = sb("s_act", [P, T])
        s_prod = sb("s_prod", [P, T])
        p_tok = sb("p_tok", [P, NT, DP])
        ps_tok = sb("ps_tok", [NS, DP])
        ident = sb("ident", [P, P])
        ones = sb("ones", [P, P])
        head_ones = sb("head_ones", [P, P])
        from_here = sb("from_here", [P, P])
        not_before = sb("not_before", [P, P])
        gains = sb("gains", [P, VECS])
        taps = sb("taps", [P, TAPS * KD])
        qk_gain = sb("qk_gain", [P, 2])
        bias = sb("bias", [P, NH])
        eps = sb("eps", [P, 2])
        pages = sb("pages", [1, NS * PG], I32)

        def phase_memory(*specs):
            with ExitStack() as stack:
                return [stack.enter_context(nc.sbuf_tensor(n, s, d)) for n, s, d in specs]

        x_tok, xs_tok, vec_rows, tap_rows = phase_memory(
            ("x_tok", [P, NT, D], F32), ("xs_tok", [NS, D], F32), ("vec_rows", [VECS, P], F32),
            ("tap_rows", [TAPS * KD // 2, 2, P], F32))
        a_hi, a_lo = phase_memory(("a_hi", [P, KF, T], F32R), ("a_lo", [P, KF, T], F32R))
        (o_hi, o_lo, k_f, v_tok, l_b, sp_a, sp_1, run, a_b, kc, vc,
         zs, ls, sps, runs) = phase_memory(
            ("o_hi", [P, KD, T], F32R), ("o_lo", [P, KD, T], F32R), ("k_f", [P, T], F32),
            ("v_tok", [P, NT, P], F32),
            ("l_b", [P, 2, 2, TP], F32), ("sp_a", [P, 2, TP], F32), ("sp_1", [P, 2, 3 * P], F32), ("run", [P, 2, TP], F32),
            ("a_b", [P, 2 * (TP + 6 * P)], F32), ("kc", [P, PG, D], F32), ("vc", [P, PG, D], F32),
            ("zs", [P, PG, 2 * NS], F32), ("ls", [P, PG, 2 * NS], F32),
            ("sps", [P, PG, 2 * NS], F32), ("runs", [P, PG, 2 * NS], F32))
        q_all, = phase_memory(("q_all", [P, KD, T], F32))
        g_pad, tap_now, tap_prods, tap_sum, tap_own, g_last, st_rows, st, y, c_hi, c_lo, cv_tok = phase_memory(
            ("g_pad", [P, 2, PAD + TP], F32), ("tap_now", [P, 2, TAPS], F32), ("tap_prods", [P, RING, TP], F32),
            ("tap_sum", [P, 2, TP], F32), ("tap_own", [P, 2, TP], F32), ("g_last", [P, KD, PAD + NS], F32), ("st_rows", [4 * PAD, 2, D], F32),
            ("st", [P, KD, NS, PAD], F32), ("y", [P, KD, T], F32), ("c_hi", [P, KD, T], F32R),
            ("c_lo", [P, KD, T], F32R), ("cv_tok", [PAD + NS, D], F32))
        p_hi, p_lo, pp, out_tok, outs_tok = phase_memory(
            ("p_hi", [P, KP, T], F32R), ("p_lo", [P, KP, T], F32R), ("pp", [P, KD, T], F32),
            ("out_tok", [P, 2, NT, P], F32), ("outs_tok", [NS, D], F32))

        ps = ctx.enter_context(nc.psum_tensor("ps", [P, 4, 2, 512], F32))

        q_f = sumsq
        q_raw, k_raw, v_f, qk_r = s_gate, s_up, s_act, s_prod
        k_tok = log_ms[:, 0:TP].rearrange("p (n f) -> p n f", n=NT)
        kvs_tok = square[0:NS, 1, 0:2 * P].rearrange("p (c f) -> p c f", c=2)
        q_bc = run[:, :, :].rearrange("p e t -> p (e t)")
        q_diag = l_b[:, 1, :, :].rearrange("p e t -> p (e t)")

        def halves(ap):
            return ap.rearrange("p (b n) -> p b n", b=2)

        def slot(s):
            return ps[:, s, :, 0:HALF]

        def flat(s, b=0):
            return ps[:, s, b, :]

        slab_in = [sem("slab_in0"), sem("slab_in1")]
        slab_hi = sem("slab_hi")
        slab_lo = sem("slab_lo")
        slab_used = sem("slab_used")
        evac = sem("evac")
        h_hi_ok = sem("h_hi_ok")
        h_lo_ok = sem("h_lo_ok")
        sq_ok = sem("sq_ok")
        acc_ok = sem("acc_ok")
        stat_mm = sem("stat_mm")
        log_ok = sem("log_ok")
        rms_ok = sem("rms_ok")
        act_fn = sem("act_fn")
        prod_ok = sem("prod_ok")
        a_hi_ok = sem("a_hi_ok")
        a_lo_ok = sem("a_lo_ok")
        const_ok = sem("const_ok")
        const_set = sem("const_set")
        first_in = [sem(f"first_in{n}") for n in range(6)]
        load_t = sem("load_t")
        vec_t = sem("vec_t")
        vec_ok = sem("vec_ok")
        p_in = sem("p_in")
        p_t = sem("p_t")
        p_hi_ok = sem("p_hi_ok")
        p_lo_ok = sem("p_lo_ok")
        pp_mm = sem("pp_mm")
        pp_ok = sem("pp_ok")
        prod_x = sem("prod_x")
        x_new = sem("x_new")

        at = {}
        slab = tile = norm = hid = xt = fn = pr = 0
        for layer in range(2):
            for name in (("load",) if layer == 0 else ()) + ("up1", "down1", "mix", "mixout", "up2", "down2", "ple"):
                at[name, layer] = dict(slab=slab, tile=tile, norm=norm, hid=hid, xt=xt, fn=fn)
                if name == "load":
                    tile += KD
                    xt += KD
                if name[:2] == "up":
                    slab += 2 * KF
                    tile += 2 * KF
                    fn += KF
                    hid += KF
                    norm += 1
                if name[:4] == "down":
                    slab += 2 * KD
                    tile += KD
                    xt += KD
                if name == "mix":
                    n = 3 * NP if layer == 0 else 2 * KD
                    slab += n
                    tile += n
                    fn += 0 if layer == 0 else KD
                    norm += 1
                if name == "mixout":
                    slab += KD
                    tile += KD
                    xt += KD
                if name == "ple":
                    slab += 2 + KD
                    tile += 2 * KD
                    fn += KD
                    xt += KD if layer == 0 else 0
                    norm += 1

        def gain_col(layer, which, m):
            return gains[:, ds((layer * 4 + which) * KD + m, 1)]

        def load_slab(sp, n, j, src, kt):
            sp.wait_ge(slab_lo, n - 1)
            dst = w_raw[:, j, 0:kt * P].rearrange("p (k c) -> p k c", k=kt)
            sp.dma_start(dst, src).then_inc(slab_in[j], 16)

        def split_hi(act, n, half, j, cols=KD * P):
            act.wait_ge(slab_in[j], 16 * half + 16)
            act.wait_ge(slab_used, n - 1)
            act.activation(w_hi[:, j, 0:cols], w_raw[:, j, 0:cols], ACT.Copy).then_inc(slab_hi, 1)

        def split_lo(dve, n, j, cols=KD * P):
            dve.wait_ge(slab_hi, n + 1)
            dve.tensor_tensor(w_lo[:, j, 0:cols], w_raw[:, j, 0:cols], w_hi[:, j, 0:cols].bitcast(F32),
                              ALU.subtract).then_inc(slab_lo, 1)

        def products(pe, out, j, w0, kts, hi, lo, k0, first, last, wait_k=None):
            for k in kts:
                if wait_k is not None:
                    wait_k(k)
                w = slice(w0 + k * P, w0 + (k + 1) * P)
                for n, (a, b) in enumerate(((w_hi, hi), (w_hi, lo), (w_lo, hi))):
                    for b_ in range(2):
                        ins = pe.matmul(out[:, b_, :], a[:, j, w], b[:, k0 + k, b_ * HALF:(b_ + 1) * HALF],
                                        start=(first and k == kts[0] and n == 0),
                                        stop=(last and k == kts[-1] and n == 2))
            return ins

        def x_post_act(act, at_, layer, which, m, m2):
            xm = x[:, ds(m, 1), :].rearrange("p a t -> p (a t)")
            if at_["xt"] or m > 1:
                act.wait_ge(acc_ok, at_["xt"] + m - 1)
            act.wait_ge(evac, at_["tile"] + m + 1)
            act.activation(h_hi[:, ds(m, 1), :].rearrange("p a t -> p (a t)"), xm, ACT.Copy,
                           scale=gain_col(layer, which, m)).then_inc(h_hi_ok, 1)
            act.activation(square[:, m2, :], xm, ACT.Square).then_inc(sq_ok, 1)

        def x_post_dve(dve, at_, layer, which, m):
            dve.wait_ge(h_hi_ok, at_["xt"] + m + 1)
            dve.scalar_tensor_tensor(h_lo[:, ds(m, 1), :].rearrange("p a t -> p (a t)"),
                                     x[:, ds(m, 1), :].rearrange("p a t -> p (a t)"), gain_col(layer, which, m),
                                     h_hi[:, ds(m, 1), :].rearrange("p a t -> p (a t)").bitcast(F32),
                                     ALU.mult, ALU.subtract).then_inc(h_lo_ok, 1)

        def x_add_pool(pool, at_, m, m2, first=False):
            pool.wait_ge(sq_ok, at_["xt"] + m + 1)
            if first:
                if at_["norm"]:
                    pool.wait_ge(stat_mm, at_["norm"])
                pool.tensor_copy(sumsq[:, :], square[:, m2, :]).then_inc(acc_ok, 1)
            else:
                pool.wait_ge(acc_ok, at_["xt"] + m)
                pool.tensor_tensor(sumsq[:, :], sumsq[:, :], square[:, m2, :], ALU.add).then_inc(acc_ok, 1)

        def stat_pe(pe, a):
            pe.wait_ge(acc_ok, a["xt"])
            for b in range(2):
                ins = pe.matmul(ps[:, 3, b, 0:HALF], ones[:, :], sumsq[:, b * HALF:(b + 1) * HALF],
                                start=True, stop=True)
            ins.then_inc(stat_mm, 1)

        def stat_act(act, a):
            act.preload_act_table_set(LOG_EXP)
            act.wait_ge(stat_mm, a["norm"] + 1)
            act.activation(halves(log_ms[:, :]), slot(3), ACT.Ln, scale=1.0 / D, bias=eps[:, 0:1]).then_inc(log_ok, 1)
            act.wait_ge(log_ok, a["norm"] + 1)
            act.activation(rms[:, :], log_ms[:, :], ACT.Exp, scale=-0.5).then_inc(rms_ok, 1)

        def scaled(dve, out, s, n):
            dve.wait_ge(slab_used, n + 1)
            dve.tensor_tensor(halves(out), slot(s), halves(rms[:, :]), ALU.mult).then_inc(evac, 1)

        def add_to_x(dve, s, n, m, factor):
            dve.wait_ge(slab_used, n + 1)
            xm = x[:, ds(m, 1), :].rearrange("p a (b n) -> p (a b) n", b=2)
            dve.scalar_tensor_tensor(xm, slot(s), factor, xm, ALU.mult, ALU.add).then_inc(evac, 1)

        def slab_src(w, m, k0=0, kt=KD):
            return w.rearrange("(k p) f -> p k f", p=P)[:, k0:k0 + kt, ds(m * P, P)]

        def up_sp(sp, a, layer, wg, wu):
            n0 = a["slab"]
            if n0 == 0:
                for j, w in ((0, wg), (1, wu)):
                    sp.dma_start(w_raw[:, j, 0:KD * P].rearrange("p (k c) -> p k c", k=KD),
                                 slab_src(w[layer], 0)).then_inc(slab_in[j], 16)
            with sp.Fori(1 if n0 == 0 else 0, KF) as f:
                for j, w in ((0, wg), (1, wu)):
                    load_slab(sp, n0 + 2 * f + j, j, slab_src(w[layer], f), KD)

        def silu_act(act, a, f):
            act.wait_ge(evac, a["tile"] + 2 * f + 1)
            act.activation(s_act[:, :], s_gate[:, :], ACT.Silu).then_inc(act_fn, 1)

        def hidden_hi_act(act, a, f):
            act.wait_ge(prod_ok, a["hid"] + f + 1)
            act.activation(a_hi[:, ds(f, 1), :].rearrange("p a t -> p (a t)"), s_prod[:, :],
                           ACT.Copy).then_inc(a_hi_ok, 1)

        def hidden_dve(dve, a, f):
            dve.wait_ge(act_fn, a["fn"] + f + 1)
            dve.wait_ge(evac, a["tile"] + 2 * f + 2)
            dve.tensor_tensor(s_prod[:, :], s_act[:, :], s_up[:, :], ALU.mult).then_inc(prod_ok, 1)
            dve.wait_ge(a_hi_ok, a["hid"] + f + 1)
            dve.tensor_tensor(a_lo[:, ds(f, 1), :].rearrange("p a t -> p (a t)"), s_prod[:, :],
                              a_hi[:, ds(f, 1), :].rearrange("p a t -> p (a t)").bitcast(F32),
                              ALU.subtract).then_inc(a_lo_ok, 1)

        def up_act(act, a, prev):
            n0 = a["slab"]
            for j in range(2):
                if n0:
                    split_hi(act, n0 + j, n0 // 2, j)
                else:
                    act.wait_ge(slab_in[j], 16)
                    act.activation(w_hi[:, j, 0:D], w_raw[:, j, 0:D], ACT.Copy).then_inc(slab_hi, 1)
                prev(j)
            for f in range(1, 2):
                split_hi(act, n0 + 2 * f, n0 // 2 + f, 0)
                stat_act(act, a)
                silu_act(act, a, f - 1)
                split_hi(act, n0 + 2 * f + 1, n0 // 2 + f, 1)
                hidden_hi_act(act, a, f - 1)
            with act.Fori(2, KF) as f:
                split_hi(act, n0 + 2 * f, n0 // 2 + f, 0)
                silu_act(act, a, f - 1)
                split_hi(act, n0 + 2 * f + 1, n0 // 2 + f, 1)
                hidden_hi_act(act, a, f - 1)

        def up_dve(dve, a, prev_evac, prev_lo):
            n0, t0 = a["slab"], a["tile"]
            for j in range(2):
                prev_evac(j)
                split_lo(dve, n0 + j, j)
                prev_lo(j)

            def step(f, s):
                scaled(dve, s_gate[:, :], s, n0 + 2 * f - 2)
                split_lo(dve, n0 + 2 * f, 0)
                scaled(dve, s_up[:, :], s + 1, n0 + 2 * f - 1)
                split_lo(dve, n0 + 2 * f + 1, 1)
                hidden_dve(dve, a, f - 1)

            dve.wait_ge(rms_ok, a["norm"] + 1)
            step(1, 0)
            with dve.Fori(1, KF // 2) as half:
                f = 2 * half
                step(f, 2)
                step(f + 1, 0)

        def up_pe(pe, a):
            n0, t0 = a["slab"], a["tile"]

            def gate_or_up(f, c, s, wait_h=False, free=None):
                pe.wait_ge(slab_lo, n0 + 2 * f + c + 1)
                pe.wait_ge(evac, t0 + 2 * f + c - 3 if free is None else free)
                wait_k = (lambda k: pe.wait_ge(h_lo_ok, a["xt"] - KD + k + 1)) if wait_h else None
                ins = products(pe, slot(s), c, 0, range(KD), h_hi, h_lo, 0, True, True, wait_k)
                ins.then_inc(slab_used, 1)

            gate_or_up(0, 0, 0, True, t0 - 1)
            pe.wait_ge(evac, t0)
            stat_pe(pe, a)
            gate_or_up(0, 1, 1, False, t0)
            gate_or_up(1, 0, 2, False, t0)
            pe.wait_ge(rms_ok, a["norm"] + 1)
            gate_or_up(1, 1, 3, False, t0)
            with pe.Fori(1, KF // 2) as half:
                f = 2 * half
                gate_or_up(f, 0, 0)
                gate_or_up(f, 1, 1)
                gate_or_up(f + 1, 0, 2)
                gate_or_up(f + 1, 1, 3)

        def to_x_sp(sp, a, spt, w):
            n0 = a["slab"]
            with sp.Fori(0, KD * spt // 2) as step:
                m = 2 // spt * step
                for j in range(2):
                    src = slab_src(w, m, j * KH, KH) if spt == 2 else slab_src(w, m + j)
                    load_slab(sp, n0 + spt * m + j, j, src, KH if spt == 2 else KD)

        def to_x_act(act, a, spt, layer, which, prev):
            n0, cols = a["slab"], (KH if spt == 2 else KD) * P
            for j in range(2):
                split_hi(act, n0 + j, n0 // 2, j, cols)
                prev(j)

            def post(m, m2):
                x_post_act(act, a, layer, which, m, m2)

            if spt == 2:
                def step(m, m2):
                    split_hi(act, n0 + 2 * m, n0 // 2 + m, 0, cols)
                    split_hi(act, n0 + 2 * m + 1, n0 // 2 + m, 1, cols)
                    post(m - 1, m2)
                step(1, 0)
                with act.Fori(1, KD // 2) as half:
                    m = 2 * half
                    step(m, 1)
                    step(m + 1, 0)
            else:
                with act.Fori(1, KD // 2) as u:
                    for j in range(2):
                        split_hi(act, n0 + 2 * u + j, n0 // 2 + u, j, cols)
                        post(2 * u + j - 2, j)

        def to_x_dve(dve, a, spt, layer, which, factor, prev_evac, prev_lo):
            n0, cols = a["slab"], (KH if spt == 2 else KD) * P
            for j in range(2):
                prev_evac(j)
                split_lo(dve, n0 + j, j, cols)
                prev_lo(j)
            if spt == 2:
                def step(m, s):
                    split_lo(dve, n0 + 2 * m, 0, cols)
                    add_to_x(dve, s, n0 + 2 * m - 1, m - 1, factor)
                    split_lo(dve, n0 + 2 * m + 1, 1, cols)
                    x_post_dve(dve, a, layer, which, m - 1)
                step(1, 0)
                with dve.Fori(1, KD // 2) as half:
                    m = 2 * half
                    step(m, 1)
                    step(m + 1, 0)
            else:
                with dve.Fori(1, KD // 2) as half:
                    m = 2 * half
                    for j in range(2):
                        add_to_x(dve, j, n0 + m + j - 2, m + j - 2, factor)
                        split_lo(dve, n0 + m + j, j, cols)
                        x_post_dve(dve, a, layer, which, m + j - 2)

        def add_squares_pool(pool, a):
            x_add_pool(pool, a, 0, 0, True)
            x_add_pool(pool, a, 1, 1)
            with pool.Fori(1, KD // 2) as half:
                m = 2 * half
                x_add_pool(pool, a, m, 0)
                x_add_pool(pool, a, m + 1, 1)

        def to_x_pe(pe, a, spt, hi, lo, in_sem, in_base, in_count):
            n0, t0 = a["slab"], a["tile"]
            with pe.Fori(0, KD // 2) as half:
                m = 2 * half
                for s in range(2):
                    pe.wait_ge(evac, t0 + m + s - 1)
                    for c in range(spt):
                        j = c if spt == 2 else s
                        pe.wait_ge(slab_lo, n0 + spt * (m + s) + c + 1)
                        pe.wait_ge(in_sem, in_base + (in_count // spt) * (c + 1))
                        kts = range(KH if spt == 2 else KD)
                        products(pe, slot(s), j, 0, kts, hi, lo, c * KH, c == 0, c == spt - 1).then_inc(slab_used, 1)

        L = at["load", 0]

        def load_sp(sp):
            sp.dma_start(x_tok[:, :, :], io["x_prompt"][0].rearrange("(n p) f -> p n f", p=P)).then_inc(first_in[0], 16)
            sp.dma_start(xs_tok[:, :], io["x_sample"].rearrange("b a f -> (b a) f")).then_inc(first_in[0], 16)
            for layer in range(2):
                for which, name in enumerate(NORMS):
                    r = (layer * 4 + which) * KD
                    sp.dma_start(vec_rows[r:r + KD, :], io[name][layer].rearrange("(k p) -> k p", p=P)).then_inc(first_in[1], 16)
            for c, name in enumerate(("conv_b_dw", "conv_ln_g", "conv_ln_b")):
                r = (8 + c) * KD
                sp.dma_start(vec_rows[r:r + KD, :], io[name][0].rearrange("(k p) -> k p", p=P)).then_inc(first_in[1], 16)
            sp.dma_start(tap_rows[:, :, :], io["conv_w_dw"][0].rearrange("w (k p) -> (w k) p", p=P).rearrange(
                "(a r) p -> r a p", a=2)).then_inc(first_in[1], 16)
            for half in range(2):
                for c, name in enumerate(("attn_q_norm", "attn_k_norm")):
                    sp.dma_start(qk_gain[half * HD:(half + 1) * HD, c:c + 1],
                                 io[name].rearrange("a d -> d a")).then_inc(first_in[2], 16)
            sp.dma_start(bias[0:1, :], io["attn_logit_bias"]).then_inc(first_in[2], 16)
            sp.dma_start(pages[:, :], io["page_table"].rearrange("(a b) g -> a (b g)", a=1)).then_inc(first_in[3], 16)
            load_p(sp, 0)

        def load_p(sp, layer):
            sp.dma_start(p_tok[:, :, :], io["p_prompt"][layer, 0].rearrange("(n p) f -> p n f", p=P)).then_inc(p_in, 16)
            sp.dma_start(ps_tok[:, :], io["p_sample"][layer].rearrange("b a f -> (b a) f")).then_inc(p_in, 16)

        def load_pool(pool):
            for t, v in ((ones, 1.0), (ident, 0.0), (from_here, 0.0), (not_before, 0.0), (head_ones, 0.0)):
                pool.memset(t[:, :], v).then_inc(const_set, 1)
            pool.memset(eps[:, 0:1], EPS).then_inc(const_set, 1)
            pool.memset(eps[:, 1:2], LN_EPS).then_inc(const_set, 1)
            pool.wait_ge(const_set, 7)
            for t, keep, fill in ((ident, ALU.not_equal, 1.0), (from_here, ALU.is_gt, 1.0), (not_before, ALU.is_gt, -1e30)):
                pool.affine_select(out=t[:, :], in_=t[:, :], compare_op=keep, fill=fill, base=0,
                                   pattern=[[1, P]], channel_multiplier=-1).then_inc(const_ok, 1)
            for n, r in enumerate((0, HD)):
                pool.wait_ge(const_ok, 3 + n)
                pool.memset(head_ones[r:r + HD, r:r + HD], 1.0).then_inc(const_ok, 1)

        def load_pe(pe):
            pe.wait_ge(const_ok, 5)
            pe.wait_ge(first_in[1], 16 * 12)
            pe.transpose(ps[:, 2, 0, 0:VECS], vec_rows[:, :], ident[0:VECS, 0:VECS])
            R = TAPS * KD // 2
            for c in range(2):
                pe.transpose(ps[:, 2, 0, VECS + c * R:VECS + (c + 1) * R], tap_rows[:, c, :], ident[0:R, 0:R])
            pe.wait_ge(first_in[2], 16 * 5)
            pe.matmul(ps[:, 2, 1, 0:NH], ones[0:1, :], bias[0:1, :], start=True, stop=True).then_inc(vec_t, 1)
            pe.wait_ge(first_in[0], 32)
            for m in range(KD):
                if m >= 2:
                    pe.wait_ge(evac, m - 1)
                for n in range(NT):
                    pe.transpose(ps[:, m % 2, 0, n * P:(n + 1) * P], x_tok[:, n, m * P:(m + 1) * P], ident[:, :])
                pe.transpose(ps[:, m % 2, 1, 0:NS], xs_tok[:, m * P:(m + 1) * P], ident[0:NS, 0:NS]).then_inc(load_t, 1)

        def load_dve(dve):
            dve.wait_ge(vec_t, 1)
            dve.tensor_copy(gains[:, :], ps[:, 2, 0, 0:VECS]).then_inc(vec_ok, 1)
            dve.tensor_copy(taps[:, :], ps[:, 2, 0, VECS:VECS + TAPS * KD]).then_inc(vec_ok, 1)
            dve.tensor_copy(bias[:, :], ps[:, 2, 1, 0:NH]).then_inc(vec_ok, 1)
            dve.tensor_scalar(qk_gain[:, 0:1], qk_gain[:, 0:1], HD ** -0.5, None, ALU.mult).then_inc(vec_ok, 1)
            for m in range(KD):
                dve.wait_ge(load_t, m + 1)
                dve.tensor_copy(x[:, m, 0:TP], ps[:, m % 2, 0, :])
                dve.tensor_copy(x[:, m, TP:T], ps[:, m % 2, 1, 0:NS]).then_inc(evac, 1)
                if m >= 1:
                    x_post_dve(dve, L, 0, 0, m - 1)

        def load_act(act):
            act.wait_ge(vec_ok, 4)
            for m in range(KD - 1):
                x_post_act(act, L, 0, 0, m, m % 2)

        def nothing(j):
            pass

        def after_to_x(a, spt, layer, which, factor):
            def act_part(act):
                def run_(j):
                    m = KD - 2 + j
                    if spt == 1 or j == 1:
                        x_post_act(act, a, layer, which, m, m % 2)
                return run_

            def dve_evac(dve):
                def run_(j):
                    m = KD - 2 + j
                    if spt == 1 or j == 1:
                        add_to_x(dve, m % 2, a["slab"] + spt * (m + 1) - 1, m, factor)
                return run_

            def dve_lo(dve):
                def run_(j):
                    if spt == 1 or j == 1:
                        x_post_dve(dve, a, layer, which, KD - 2 + j)
                return run_
            return act_part, dve_evac, dve_lo

        def after_up(a):
            def act_part(act):
                return lambda j: (silu_act, hidden_hi_act)[j](act, a, KF - 1)

            def dve_evac(dve):
                return lambda j: scaled(dve, (s_gate, s_up)[j][:, :], 2 + j, a["slab"] + 2 * KF - 2 + j)

            def dve_lo(dve):
                return lambda j: hidden_dve(dve, a, KF - 1) if j else None
            return act_part, dve_evac, dve_lo

        def after_load():
            def act_part(act):
                def run_(j):
                    if j == 0:
                        x_post_act(act, L, 0, 0, KD - 1, 1)
                return run_
            return act_part, (lambda dve: nothing), (lambda dve: lambda j: x_post_dve(dve, L, 0, 0, KD - 1) if j == 0 else None)

        M = at["mix", 0]
        mix_in = [sem("k_cache_in"), sem("v_cache_in")]
        q_here = sem("q_here")
        sq_qk = sem("sq_qk")
        head_mm = sem("head_mm")
        head_log = sem("head_log")
        head_r = sem("head_r")
        qk_ok = sem("qk_ok")
        diag_ok = sem("diag_ok")
        kt_mm = sem("kt_mm")
        vt_mm = sem("vt_mm")
        kt_ok = sem("kt_ok")
        vt_ok = sem("vt_ok")
        k_out = sem("k_out")
        v_out = sem("v_out")
        bc_mm = sem("bc_mm")
        bc_ok = sem("bc_ok")
        kq_ok = sem("kq_ok")
        z_mm = sem("z_mm")
        z_ok = sem("z_ok")
        abs_ok = sem("abs_ok")
        sp_ok = sem("sp_ok")
        run_ok = sem("run_ok")
        c_mm = sem("c_mm")
        t_ok = sem("t_ok")
        w_ok = sem("w_ok")
        o_mm = sem("o_mm")
        o_hi_ok = sem("o_hi_ok")
        os_ok = sem("os_ok")
        zs_ok = sem("zs_ok")
        ls_ok = sem("ls_ok")
        cs_mm = sem("cs_mm")
        os_mm = sem("os_mm")

        FIRST = (P, P, 0)
        STAGE_AT = (0, 2 * 3 * P, 4 * 3 * P)
        TILES = (((2, P, 2 * P), (3, 3 * P, 3 * P)), ((1, P, P),), ((0, 0, 0),))

        def stage(st):
            w = TP - FIRST[st]
            return a_b[:, STAGE_AT[st]:STAGE_AT[st] + 2 * w].rearrange("p (e t) -> p e t", e=2)

        def l_of(st):
            return l_b[:, st % 2, :, FIRST[st]:TP]

        def sp_of(st):
            return sp_1[:, :, :] if st == 1 else sp_a[:, :, FIRST[st]:TP]

        def qkv_src(c, hp):
            return io["attn_w_qkv"][0].rearrange("(k p) f -> p k f", p=P)[:, :, ds(c * D + hp * P, P)]

        q_at = lambda m: (s_gate, s_up)[m % 2]
        r_at = lambda m: (s_act, s_prod)[m % 2]

        def attn_sp(sp):
            n0 = M["slab"]

            def kv(hp):
                for c in range(2):
                    load_slab(sp, n0 + NP + 2 * hp + c, c, qkv_src(1 + c, hp), KD)

            def cache(c, b):
                for g in range(PG):
                    page = sp.value_load(pages[0:1, b * PG + g:b * PG + g + 1], min_val=0,
                                         max_val=io["cache_k"].shape[1] - 1)
                    rows = io[("cache_k", "cache_v")[c]][0].rearrange("n p h d -> n p (h d)")[ds(page, 1), :, :]
                    sp.dma_start((kc, vc)[c][:, g, :], rows.rearrange("a p f -> p (a f)")).then_inc(mix_in[c], 16)

            for m in range(NP):
                load_slab(sp, n0 + m, m % 2, qkv_src(0, m), KD)
            sp.wait_ge(first_in[3], 16)
            sp.wait_ge(slab_used, n0)
            cache(0, 0)
            cache(1, 0)
            kv(0)
            kv(1)
            for hp in range(NP - 1):
                if hp + 2 < NP:
                    kv(hp + 2)
                sp.wait_ge(zs_ok, 9 * hp + 4)
                cache(0, hp + 1)
                sp.wait_ge(os_mm, hp + 1)
                cache(1, hp + 1)

        def attn_pe(pe):
            n0, t0 = M["slab"], M["tile"]

            def part(n, j, s, kts, wait_k=None):
                return products(pe, slot(s), j, 0, kts, h_hi, h_lo, 0, kts[0] == 0, kts[-1] == KD - 1, wait_k)

            def whole(n, j, wait_k=None):
                pe.wait_ge(slab_lo, n + 1)
                pe.wait_ge(evac, t0 - n0 + n - 1)
                part(n, j, j, range(KD), wait_k).then_inc(slab_used, 1)

            def head_sums(m, c, s):
                pe.wait_ge(sq_qk, m + 1)
                for b in range(2):
                    ins = pe.matmul(ps[:, s, b, 0:HALF], head_ones[:, :], square[:, c, b * HALF:(b + 1) * HALF],
                                    start=True, stop=True)
                ins.then_inc(head_mm, 1)

            whole(n0, 0, lambda k: pe.wait_ge(h_lo_ok, M["xt"] - KD + k + 1))
            pe.wait_ge(evac, t0)
            stat_pe(pe, M)
            whole(n0 + 1, 1)
            head_sums(0, 0, 2)
            whole(n0 + 2, 0)
            pe.wait_ge(rms_ok, M["norm"] + 1)
            head_sums(1, 1, 3)
            whole(n0 + 3, 1)
            pe.wait_ge(head_log, 1)
            head_sums(2, 0, 2)
            with pe.Fori(2, NP // 2) as half:
                for j in range(2):
                    m = 2 * half + j
                    whole(n0 + m, j)
                    pe.wait_ge(head_log, m - 2)
                    head_sums(m - 1, 1 - j, 3 - j)

            def transposed(src, s, done):
                for n in range(NT):
                    pe.transpose(ps[:, s, 0, n * P:(n + 1) * P], src[:, n * P:(n + 1) * P], ident[:, :])
                pe.transpose(ps[0:NS, s, 1, 0:P], src[:, TP:T], ident[:, :]).then_inc(done, 1)

            def k_sums(hp):
                pe.wait_ge(head_log, NP + hp)
                head_sums(NP + hp, 0, 2)

            def k_turned(hp):
                pe.wait_ge(head_log, NP + hp + 1)
                pe.wait_ge(qk_ok, NP + hp + 1)
                transposed(k_f, 2, kt_mm)

            def v_turned(hp):
                pe.wait_ge(kt_ok, 2 * hp + 2)
                pe.wait_ge(evac, t0 + NP + 2 * hp + 2)
                transposed(v_f, 2, vt_mm)

            def q_spread(b):
                pe.wait_ge(diag_ok, b + 1)
                for c in range(2):
                    ins = pe.matmul(ps[:, 3, c, :], ones[:, :], q_diag[:, c * TP:(c + 1) * TP], start=True, stop=True)
                ins.then_inc(bc_mm, 1)

            def pair(hp, more):
                def chunk(c):
                    if not more:
                        return
                    s = c // 4
                    n = n0 + NP + 2 * hp + 2 + s
                    if c % 4 == 0:
                        pe.wait_ge(slab_lo, n + 1)
                        pe.wait_ge(evac, t0 + NP + 2 * hp + 1 + s)
                    ins = part(n, s, s, range(c % 4 * 2, c % 4 * 2 + 2))
                    if c % 4 == 3:
                        ins.then_inc(slab_used, 1)

                def scores(st):
                    if st == 0:
                        pe.wait_ge(q_here, hp + 1)
                        pe.wait_ge(vt_ok, 2 * hp + 2)
                    else:
                        pe.wait_ge(z_ok, 3 * hp + st)
                    for i, c, t in TILES[st]:
                        for hd in range(2):
                            r = slice(hd * HD, hd * HD + HD)
                            ins = pe.matmul(ps[:, 2, hd, c:c + TP - t], k_f[r, i * P:(i + 1) * P], q_f[r, t:TP],
                                            start=True, stop=True)
                    ins.then_inc(z_mm, 1)

                def later_sum(st):
                    pe.wait_ge(sp_ok, 3 * hp + st + 1)
                    if st:
                        pe.wait_ge(t_ok, 3 * hp + st)
                        pe.wait_ge(run_ok, 2 * hp + st)
                    elif not isinstance(hp, int) or hp:
                        pe.wait_ge(os_ok, 3 * hp)
                    for hd in range(2):
                        pe.matmul(ps[:, 3, hd, FIRST[st]:TP], from_here[:, :], sp_of(st)[:, hd, :],
                                  start=True, stop=False)
                        old = 2 * P * (st < 2) + P * (st == 2)
                        if st == 0:
                            ins = pe.matmul(ps[:, 3, hd, 2 * P:3 * P], ones[:, :], sp_a[:, hd, 3 * P:TP],
                                            start=False, stop=True)
                        else:
                            ins = pe.matmul(ps[:, 3, hd, old:TP], ones[:, :], run[:, hd, old:TP],
                                            start=False, stop=True)
                    ins.then_inc(c_mm, 1)

                scores(0)
                chunk(0)
                scores(1)
                chunk(1)
                scores(2)
                later_sum(0)
                chunk(2)
                later_sum(1)
                chunk(3)
                later_sum(2)
                chunk(4)
                pe.wait_ge(t_ok, 3 * hp + 3)
                if more:
                    q_spread(hp + 1)
                    pe.wait_ge(z_ok, 3 * hp + 3)
                    k_sums(hp + 1)
                chunk(5)
                chunk(6)
                if more:
                    pe.wait_ge(bc_ok, hp + 2)
                pe.wait_ge(w_ok, 3 * hp + 3)
                for hd in range(2):
                    for st in (2, 1, 0):
                        for i, c, t in TILES[st]:
                            c -= FIRST[st]
                            ins = pe.matmul(ps[hd * HD:(hd + 1) * HD, 3, 0, t:TP], v_tok[:, i, hd * HD:(hd + 1) * HD],
                                            stage(st)[:, hd, c:c + TP - t], start=i == 0, stop=i == 3)
                ins.then_inc(o_mm, 1)
                pe.wait_ge(zs_ok, 9 * hp + 8)
                pe.matmul(ps[:, 3, 1, 0:PG * NH], from_here[:, :], sps[:, :, :].rearrange("p g c -> p (g c)"),
                          start=True, stop=False)
                pe.matmul(ps[:, 3, 1, 0:(PG - 1) * NH], ones[:, :],
                          runs[:, 0:PG - 1, :].rearrange("p g c -> p (g c)"), start=False, stop=True).then_inc(cs_mm, 1)
                if more:
                    k_turned(hp + 1)
                chunk(7)
                pe.wait_ge(ls_ok, 4 * hp + 4)
                pe.wait_ge(mix_in[1], 16 * PG * (hp + 1))
                for k in range(KD):
                    for g in range(PG):
                        ins = pe.matmul(ps[:, 3, 1, 2 * k:2 * k + 2], vc[:, g, k * P:(k + 1) * P], zs[:, g, 2 * k:2 * k + 2],
                                        start=g == 0, stop=g == PG - 1)
                ins.then_inc(os_mm, 1)
                if more:
                    v_turned(hp + 1)

            whole(n0 + NP, 0)
            pe.wait_ge(head_log, NP - 2)
            head_sums(NP - 1, 1, 3)
            whole(n0 + NP + 1, 1)
            k_sums(0)
            pe.wait_ge(head_log, NP)
            q_spread(0)
            k_turned(0)
            v_turned(0)
            pair(0, True)
            with pe.Fori(1, NP - 1) as hp:
                pair(hp, True)
            pair(NP - 1, False)

        def attn_act(act, prev):
            n0, t0 = M["slab"], M["tile"]

            def squares(m, src, c, t):
                act.wait_ge(evac, t + 1)
                act.activation(square[:, c, :], src[:, :], ACT.Square).then_inc(sq_qk, 1)

            def factor(m, s, dst):
                if not isinstance(m, int) or m:
                    act.wait_ge(head_r, m)
                act.wait_ge(head_mm, m + 1)
                act.activation(halves(log_ms[:, :]), slot(s), ACT.Ln, scale=1.0 / HD, bias=eps[:, 0:1]).then_inc(head_log, 1)
                act.wait_ge(head_log, m + 1)
                act.activation(dst[:, :], log_ms[:, :], ACT.Exp, scale=-0.5).then_inc(head_r, 1)

            def q_step(m, half, j):
                split_hi(act, n0 + m, n0 // 2 + half, j)
                squares(m - 2, q_at(j), j, t0 + m - 2)
                if not isinstance(m, int) or m > 2:
                    if not isinstance(m, int) or m > 4:
                        act.wait_ge(qk_ok, m - 4)
                    factor(m - 3, 3 - j, r_at(1 - j))

            for j in range(2):
                split_hi(act, n0 + j, n0 // 2, j)
                prev(j)
            stat_act(act, M)
            for m in range(2, 6):
                q_step(m, m // 2, m % 2)
            with act.Fori(3, NP // 2 + 1) as half:
                for j in range(2):
                    q_step(2 * half + j, half, j)
            act.wait_ge(qk_ok, NP - 2)
            factor(NP - 1, 3, s_prod)

            def k_squares(hp):
                squares(NP + hp, k_raw, 0, t0 + NP + 2 * hp)

            def k_factor(hp):
                act.wait_ge(qk_ok, NP + hp)
                if not isinstance(hp, int) or hp:
                    act.wait_ge(k_out, 32 * hp)
                factor(NP + hp, 2, qk_r)

            def q_copied(b):
                act.wait_ge(bc_mm, b + 1)
                if not isinstance(b, int) or b:
                    act.wait_ge(c_mm, 3 * b)
                act.activation(q_bc.rearrange("p (b t) -> p b t", b=2), ps[:, 3, :, :], ACT.Copy).then_inc(bc_ok, 1)

            def tokens(hp, c):
                dst, mm, ok, out, name = ((k_tok, kt_mm, kt_ok, k_out, "new_k"), (v_tok, vt_mm, vt_ok, v_out, "new_v"))[c]
                if not isinstance(hp, int) or hp:
                    act.wait_ge(out, 32 * hp)
                act.wait_ge(mm, hp + 1)
                act.activation(dst[:, :, :].rearrange("p n f -> p (n f)"), flat(2), ACT.Copy).then_inc(ok, 1)
                act.activation(kvs_tok[:, c, :], ps[0:NS, 2, 1, 0:P], ACT.Copy).then_inc(ok, 1)
                act.wait_ge(ok, 2 * hp + 2)
                act.dma_start(io[name + "_prompt"][0, 0].rearrange("(n p) h d -> p n (h d)", p=P)[:, :, ds(hp * P, P)],
                              dst[:, :, :]).then_inc(out, 16)
                act.dma_start(io[name + "_sample"][0].rearrange("b a h d -> b (a h d)")[:, ds(hp * P, P)],
                              kvs_tok[:, c, :]).then_inc(out, 16)

            def pair(hp, more, more2):
                def softplus(st):
                    n = 3 * hp + st
                    lb = l_of(st)
                    act.wait_ge(z_ok, n + 1)
                    if st != 1 and (not isinstance(n, int) or n):
                        act.wait_ge(sp_ok, n - (st == 2))
                    act.activation(lb, stage(st), ACT.Abs).then_inc(abs_ok, 1)
                    act.wait_ge(abs_ok, 3 * n + 1)
                    act.activation(lb, lb, ACT.Exp, scale=-1.0).then_inc(abs_ok, 1)
                    act.wait_ge(abs_ok, 3 * n + 2)
                    act.activation(lb, lb, ACT.Ln, bias=1.0).then_inc(abs_ok, 1)

                def weight(st):
                    act.wait_ge(t_ok, 3 * hp + st + 1)
                    act.activation(stage(st), stage(st), ACT.Exp).then_inc(w_ok, 1)

                softplus(0)
                softplus(1)
                softplus(2)
                weight(0)
                if more:
                    k_squares(hp + 1)
                weight(1)
                act.wait_ge(zs_ok, 9 * hp + 5)
                act.activation(ls[:, :, :], zs[:, :, :], ACT.Abs).then_inc(ls_ok, 1)
                act.wait_ge(ls_ok, 4 * hp + 1)
                act.activation(ls[:, :, :], ls[:, :, :], ACT.Exp, scale=-1.0).then_inc(ls_ok, 1)
                act.wait_ge(ls_ok, 4 * hp + 2)
                act.activation(ls[:, :, :], ls[:, :, :], ACT.Ln, bias=1.0).then_inc(ls_ok, 1)
                weight(2)
                if more2:
                    split_hi(act, n0 + NP + 2 * hp + 4, (n0 + NP) // 2 + hp + 2, 0)
                if more:
                    q_copied(hp + 1)
                    k_factor(hp + 1)
                act.wait_ge(o_mm, hp + 1)
                act.activation(o_hi[:, ds(hp, 1), 0:TP].rearrange("p a t -> p (a t)"), flat(3), ACT.Copy).then_inc(o_hi_ok, 1)
                act.wait_ge(zs_ok, 9 * hp + 9)
                act.activation(zs[:, :, :], zs[:, :, :], ACT.Exp).then_inc(ls_ok, 1)
                if more:
                    tokens(hp + 1, 0)
                act.wait_ge(os_mm, hp + 1)
                for hd in range(2):
                    act.activation(sample_at(o_hi, hd, hp), sample_out(hd), ACT.Copy).then_inc(o_hi_ok, 1)
                if more:
                    tokens(hp + 1, 1)
                if more2:
                    split_hi(act, n0 + NP + 2 * hp + 5, (n0 + NP) // 2 + hp + 2, 1)

            k_squares(0)
            q_copied(0)
            k_factor(0)
            tokens(0, 0)
            split_hi(act, n0 + NP + 2, (n0 + NP) // 2 + 1, 0)
            tokens(0, 1)
            split_hi(act, n0 + NP + 3, (n0 + NP) // 2 + 1, 1)
            pair(0, True, True)
            with act.Fori(1, NP - 2) as hp:
                pair(hp, True, True)
            pair(NP - 2, True, False)
            pair(NP - 1, False, False)

        def sample_out(hd):
            return ps[hd * HD:(hd + 1) * HD, 3, 1, 0:NH].rearrange("p (k e) -> p e k", e=2)[:, hd, :]

        def sample_at(o, hd, b):
            return o[hd * HD:(hd + 1) * HD, :, ds(TP + b, 1)].rearrange("p k a -> p (k a)")

        def attn_dve(dve, prev_evac, prev_lo):
            n0, t0 = M["slab"], M["tile"]

            def normed(m, dst, src, factor, c):
                dve.wait_ge(head_r, m + 1)
                dve.scalar_tensor_tensor(dst, src[:, :], qk_gain[:, c:c + 1], factor[:, :],
                                         ALU.mult, ALU.mult).then_inc(qk_ok, 1)

            def q_normed(m, j):
                dve.wait_ge(evac, t0 + m + 1)
                normed(m, q_all[:, ds(m, 1), :].rearrange("p a t -> p (a t)"), q_at(j), r_at(j), 0)

            def q_step(m, j):
                if not isinstance(m, int) or m > 4:
                    dve.wait_ge(qk_ok, m - 3)
                elif m == 4:
                    dve.wait_ge(qk_ok, 1)
                scaled(dve, q_at(j)[:, :], j, n0 + m - 2)
                split_lo(dve, n0 + m, j)
                if not isinstance(m, int) or m > 2:
                    q_normed(m - 3, 1 - j)

            for j in range(2):
                prev_evac(j)
                split_lo(dve, n0 + j, j)
                prev_lo(j)
            dve.wait_ge(rms_ok, M["norm"] + 1)
            for m in range(2, 6):
                q_step(m, m % 2)
            with dve.Fori(3, NP // 2 + 1) as half:
                for j in range(2):
                    q_step(2 * half + j, j)
            q_normed(NP - 1, 1)

            def k_evac(hp):
                dve.wait_ge(qk_ok, NP + hp)
                scaled(dve, k_raw[:, :], 0, n0 + NP + 2 * hp)

            def v_evac(hp):
                if not isinstance(hp, int) or hp:
                    dve.wait_ge(vt_mm, hp)
                scaled(dve, v_f[:, :], 1, n0 + NP + 2 * hp + 1)

            def diagonal(b):
                dve.tensor_tensor(q_diag.rearrange("p (k f) -> p k f", k=KD),
                                  ident[:, :].unsqueeze(1).broadcast_to([P, KD, P]),
                                  q_all[:, :, ds(TP + b, 1)].broadcast_to([P, KD, P]), ALU.mult).then_inc(diag_ok, 1)

            def ready(hp):
                dve.wait_ge(evac, t0 + NP + 2 * hp + 1)
                normed(NP + hp, k_f[:, :], k_raw, qk_r, 1)
                dve.tensor_copy(q_f[:, 0:TP], q_all[:, ds(hp, 1), 0:TP].rearrange("p a t -> p (a t)")).then_inc(q_here, 1)

            def pair(hp, more, more2):
                def biased(st):
                    if st == 0 and (not isinstance(hp, int) or hp):
                        dve.wait_ge(o_mm, hp)
                    dve.wait_ge(z_mm, 3 * hp + st + 1)
                    for hd in range(2):
                        b = bias[:, ds(2 * hp + hd, 1)]
                        for i, c, t in TILES[st]:
                            c1 = c + TP - t
                            out, z = stage(st)[:, hd, c - FIRST[st]:c1 - FIRST[st]], ps[:, 2, hd, c:c1]
                            ins = dve.scalar_tensor_tensor(out[:, 0:P], z[:, 0:P], b, not_before[:, :], ALU.add, ALU.add)
                            if i < 3:
                                ins = dve.tensor_scalar(out[:, P:], z[:, P:], b, None, ALU.add)
                    ins.then_inc(z_ok, 1)

                def softplus(st):
                    n = 3 * hp + st
                    dve.wait_ge(abs_ok, 3 * n + 3)
                    dve.wait_ge(z_ok, n + 1)
                    if st == 2:
                        dve.wait_ge(run_ok, 2 * hp + 1)
                        dve.wait_ge(c_mm, 3 * hp + 1)
                    dve.scalar_tensor_tensor(sp_of(st), stage(st), 0.0, l_of(st),
                                             ALU.max, ALU.add).then_inc(sp_ok, 1)

                def log_weight(st):
                    dve.wait_ge(c_mm, 3 * hp + st + 1)
                    dve.tensor_tensor(stage(st), stage(st), ps[:, 3, :, FIRST[st]:TP], ALU.subtract).then_inc(t_ok, 1)

                def page_scores(g):
                    dve.wait_ge(kq_ok, 4 * hp + g + 1)
                    dve.tensor_reduce(zs[:, g, :], kc[:, g, :].rearrange("p (h d) -> p h d", d=HD),
                                      AX.X, ALU.add).then_inc(zs_ok, 1)

                biased(0)
                if more:
                    split_lo(dve, n0 + NP + 2 * hp + 3, 1)
                page_scores(0)
                biased(1)
                softplus(0)
                page_scores(1)
                softplus(1)
                biased(2)
                log_weight(0)
                page_scores(2)
                log_weight(1)
                softplus(2)
                page_scores(3)
                dve.wait_ge(zs_ok, 9 * hp + 4)
                dve.tensor_tensor(zs[:, :, :], zs[:, :, :], bias[:, :].unsqueeze(1).broadcast_to([P, PG, NH]),
                                  ALU.add).then_inc(zs_ok, 1)
                if more:
                    k_evac(hp + 1)
                    diagonal(hp + 1)
                log_weight(2)
                dve.wait_ge(ls_ok, 4 * hp + 3)
                dve.scalar_tensor_tensor(sps[:, :, :], zs[:, :, :], 0.0, ls[:, :, :], ALU.max, ALU.add).then_inc(zs_ok, 1)
                dve.wait_ge(zs_ok, 9 * hp + 6)
                dve.tensor_tensor(runs[:, 1, :], sps[:, 2, :], sps[:, 3, :], ALU.add).then_inc(zs_ok, 1)
                dve.tensor_copy(runs[:, 2, :], sps[:, 3, :])
                dve.wait_ge(zs_ok, 9 * hp + 7)
                dve.tensor_tensor(runs[:, 0, :], runs[:, 1, :], sps[:, 1, :], ALU.add).then_inc(zs_ok, 1)
                if more2:
                    split_lo(dve, n0 + NP + 2 * hp + 4, 0)
                if more:
                    ready(hp + 1)
                dve.wait_ge(cs_mm, hp + 1)
                dve.tensor_tensor(zs[:, :, :].rearrange("p g c -> p (g c)"), zs[:, :, :].rearrange("p g c -> p (g c)"),
                                  ps[:, 3, 1, 0:PG * NH], ALU.subtract).then_inc(zs_ok, 1)
                dve.wait_ge(o_hi_ok, 3 * hp + 1)
                dve.tensor_tensor(o_lo[:, ds(hp, 1), 0:TP].rearrange("p a t -> p (a t)"), flat(3),
                                  o_hi[:, ds(hp, 1), 0:TP].rearrange("p a t -> p (a t)").bitcast(F32), ALU.subtract).then_inc(os_ok, 1)
                if more:
                    v_evac(hp + 1)
                dve.wait_ge(o_hi_ok, 3 * hp + 3)
                for hd in range(2):
                    dve.tensor_tensor(sample_at(o_lo, hd, hp), sample_out(hd), sample_at(o_hi, hd, hp).bitcast(F32),
                                      ALU.subtract).then_inc(os_ok, 1)

            k_evac(0)
            diagonal(0)
            v_evac(0)
            ready(0)
            split_lo(dve, n0 + NP + 2, 0)
            pair(0, True, True)
            with dve.Fori(1, NP - 2) as hp:
                pair(hp, True, True)
            pair(NP - 2, True, False)
            pair(NP - 1, False, False)

        def attn_pool(pool):
            def pair(hp):
                pool.wait_ge(bc_ok, hp + 1)
                pool.wait_ge(mix_in[0], 16 * PG * (hp + 1))
                for g in range(PG):
                    pool.tensor_tensor(kc[:, g, :], kc[:, g, :], q_bc, ALU.mult).then_inc(kq_ok, 1)
                pool.wait_ge(kq_ok, 4 * hp + 4)

                pool.wait_ge(sp_ok, 3 * hp + 1)
                pool.tensor_tensor(run[:, :, 3 * P:TP], sp_a[:, :, 2 * P:3 * P], sp_a[:, :, 3 * P:TP], ALU.add)
                pool.tensor_copy(run[:, :, 2 * P:3 * P], sp_a[:, :, P:2 * P]).then_inc(run_ok, 1)
                pool.wait_ge(sp_ok, 3 * hp + 2)
                pool.wait_ge(c_mm, 3 * hp + 2)
                pool.tensor_tensor(run[:, :, 2 * P:TP], run[:, :, 2 * P:TP], sp_1[:, :, P:], ALU.add)
                pool.tensor_copy(run[:, :, P:2 * P], sp_1[:, :, 0:P]).then_inc(run_ok, 1)

            with pool.Fori(0, NP) as hp:
                pair(hp)

        C = at["mix", 1]
        state_in = sem("state_in")
        state_mm = sem("state_mm")
        state_ok = sem("state_ok")
        g_ok = sem("g_ok")
        tap_prod = sem("tap_prod")
        tap_add = sem("tap_add")
        tap_ok = sem("tap_ok")
        y_ok = sem("y_ok")
        yp_ok = sem("yp_ok")
        yk_ok = sem("yk_ok")
        st_prod = sem("st_prod")
        ys_ok = sem("ys_ok")
        ysum_ok = sem("ysum_ok")
        ln_mm = sem("ln_mm")
        mean_ok = sem("mean_ok")
        yc_ok = sem("yc_ok")
        ysq_ok = sem("ysq_ok")
        var_ok = sem("var_ok")
        yn_ok = sem("yn_ok")
        c_fn = sem("c_fn")
        c_hi_ok = sem("c_hi_ok")
        c_lo_ok = sem("c_lo_ok")
        tail_mm = sem("tail_mm")
        tail_ok = sem("tail_ok")
        conv_out = sem("conv_out")

        def conv_sp(sp):
            n0 = C["slab"]

            def both(k):
                for c in range(2):
                    src = io["conv_w_in"][0].rearrange("(k p) f -> p k f", p=P)[:, :, ds(c * D + k * P, P)]
                    load_slab(sp, n0 + 2 * k + c, c, src, KD)
            both(0)
            both(1)
            sp.wait_ge(slab_used, n0)
            sp.dma_start(st_rows[:, :, :], io["state_conv"][0].rearrange("(a b) w f -> a (b w) f", a=2).rearrange(
                "a r f -> r a f")).then_inc(state_in, 16)
            both(2)
            sp.wait_ge(state_in, 16)
            for b in range(NS // 2):
                rows = st_rows[b * PAD + 1:(b + 1) * PAD, :, :]
                out = io["new_conv_sample"][0].rearrange("(a b) w f -> b w a f", a=2)
                sp.dma_start(out[b, 0:PAD - 1, :, :], rows).then_inc(conv_out, 16)
                both(b + 3)
            both(KD - 1)
            sp.wait_ge(tail_ok, 1)
            sp.dma_start(io["new_conv_prompt"][0, 0], cv_tok[0:PAD, :]).then_inc(conv_out, 16)
            sp.dma_start(io["new_conv_sample"][0, :, PAD - 1, :], cv_tok[PAD:, :]).then_inc(conv_out, 16)

        def conv_pe(pe):
            n0, t0 = C["slab"], C["tile"]

            def tile(k, c, wait_h=False):
                pe.wait_ge(slab_lo, n0 + 2 * k + c + 1)
                pe.wait_ge(evac, t0 + 2 * k + c - 1)
                wait_k = (lambda k: pe.wait_ge(h_lo_ok, C["xt"] - KD + k + 1)) if wait_h else None
                products(pe, slot(c), c, 0, range(KD), h_hi, h_lo, 0, True, True, wait_k).then_inc(slab_used, 1)

            tile(0, 0, True)
            pe.wait_ge(evac, t0)
            stat_pe(pe, C)
            tile(0, 1)
            tile(1, 0)
            pe.wait_ge(state_in, 16)
            R = 4 * PAD
            for s in range(2):
                if s:
                    pe.wait_ge(rms_ok, C["norm"] + 1)
                for k in range(s * 4, s * 4 + 4):
                    for a in range(2):
                        ins = pe.transpose(ps[:, 2 + s, k // 2 % 2, (k % 2) * 2 * R + a * R:(k % 2) * 2 * R + (a + 1) * R],
                                           st_rows[:, a, k * P:(k + 1) * P], ident[0:R, 0:R])
                ins.then_inc(state_mm, 1)
            tile(1, 1)
            with pe.Fori(2, KD) as k:
                tile(k, 0)
                tile(k, 1)
            pe.wait_ge(g_ok, 3 * KD)
            pe.wait_ge(state_ok, 3)
            for k in range(KD):
                ins = pe.transpose(ps[0:PAD + NS, 2, k // 4, k % 4 * P:(k % 4 + 1) * P], g_last[:, k, :], ident[:, :])
            ins.then_inc(tail_mm, 1)
            for c in range(2):
                pe.wait_ge(ysum_ok, KD * (c + 1))
                if c == 0:
                    pe.wait_ge(evac, t0 + 2 * KD)
                    pe.wait_ge(ys_ok, KD + 3)
                for b in range(2):
                    ins = pe.matmul(ps[:, c, b, 0:HALF], ones[:, :], sumsq[:, b * HALF:(b + 1) * HALF],
                                    start=True, stop=True)
                ins.then_inc(ln_mm, 1)

        def conv_act(act, prev):
            n0 = C["slab"]
            for j in range(2):
                split_hi(act, n0 + j, n0 // 2, j)
                prev(j)

            def sigmoid(k):
                act.wait_ge(evac, C["tile"] + 2 * k + 2)
                act.activation(s_act[:, :], s_gate[:, :], ACT.Sigmoid).then_inc(act_fn, 1)

            for j in range(2):
                split_hi(act, n0 + 2 + j, n0 // 2 + 1, j)
                if j == 0:
                    stat_act(act, C)
            def tap_products(k, j, part):
                act.wait_ge(g_ok, 3 * k + 2)
                for c in range(part * TAPS_ACT // 2, (part + 1) * TAPS_ACT // 2):
                    if c >= RING:
                        act.wait_ge(tap_add, (TAPS_ACT - 1) * k + max(c - RING, 1))
                    elif not isinstance(k, int) or k:
                        act.wait_ge(tap_add, (TAPS_ACT - 1) * k + c + 1 - RING)
                    w = TAPS_DVE + c
                    act.activation(tap_prods[:, (TAPS_ACT * j + c) % RING, :], g_pad[:, j, w:w + TP], ACT.Copy,
                                   scale=tap_now[:, j, w:w + 1]).then_inc(tap_prod, 1)

            def step(k, j, more):
                if more:
                    split_hi(act, n0 + 2 * k + 2, n0 // 2 + k + 1, 0)
                tap_products(k - 1, 1 - j, 0)
                sigmoid(k)
                if more:
                    split_hi(act, n0 + 2 * k + 3, n0 // 2 + k + 1, 1)
                tap_products(k - 1, 1 - j, 1)

            sigmoid(0)
            step(1, 1, True)
            with act.Fori(1, KD // 2 - 1) as half:
                for j in range(2):
                    step(2 * half + j, j, True)
            step(KD - 2, 0, True)
            step(KD - 1, 1, False)
            for part in range(2):
                tap_products(KD - 1, 1, part)
            act.wait_ge(ln_mm, 1)
            act.activation(halves(log_ms[:, :]), slot(0), ACT.Copy, scale=1.0 / D).then_inc(mean_ok, 1)
            for k in range(KD):
                act.wait_ge(yc_ok, k + 1)
                if k >= 2:
                    act.wait_ge(ysum_ok, KD + k - 1)
                act.activation(square[:, k % 2, :], y[:, k, :], ACT.Square).then_inc(ysq_ok, 1)
            act.wait_ge(tail_mm, 1)
            act.activation(cv_tok[:, :], ps[0:PAD + NS, 2, :, :].rearrange("p b t -> p (b t)"), ACT.Copy).then_inc(tail_ok, 1)
            act.preload_act_table_set(LOG_EXP)
            act.wait_ge(ln_mm, 2)
            act.activation(halves(s_gate[:, :]), slot(1), ACT.Ln, scale=1.0 / D, bias=eps[:, 1:2]).then_inc(var_ok, 1)
            act.wait_ge(var_ok, 1)
            act.activation(s_up[:, :], s_gate[:, :], ACT.Exp, scale=-0.5).then_inc(var_ok, 1)
            for k in range(KD):
                act.wait_ge(yn_ok, k + 1)
                act.activation(y[:, k, :], y[:, k, :], ACT.Silu, scale=gains[:, 9 * KD + k:9 * KD + k + 1],
                               bias=gains[:, 10 * KD + k:10 * KD + k + 1]).then_inc(c_fn, 1)
                act.wait_ge(c_fn, k + 1)
                act.activation(c_hi[:, k, :], y[:, k, :], ACT.Copy).then_inc(c_hi_ok, 1)

        def conv_dve(dve, prev_evac, prev_lo):
            n0, t0 = C["slab"], C["tile"]
            for j in range(2):
                prev_evac(j)
                split_lo(dve, n0 + j, j)
                prev_lo(j)
            dve.memset(g_pad[:, :, 0:PAD], 0.0).then_inc(state_ok, 1)
            dve.wait_ge(rms_ok, C["norm"] + 1)

            def state():
                for s in range(2):
                    dve.wait_ge(state_mm, s + 1)
                    for b in range(2):
                        ins = dve.tensor_copy(st[:, s * 4 + b * 2:s * 4 + b * 2 + 2, :, :],
                                              ps[:, 2 + s, b, 0:2 * NS * PAD].rearrange("p (k b w) -> p k b w", k=2, b=NS))
                    ins.then_inc(state_ok, 1)

            def state_sum():
                dve.wait_ge(st_prod, 1)
                dve.tensor_reduce(y[:, :, TP:T], st[:, :, :, :], AX.X, ALU.add).then_inc(ys_ok, 1)
                dve.wait_ge(ys_ok, 1)
                dve.tensor_tensor(y[:, :, TP:T], y[:, :, TP:T], gains[:, 8 * KD:9 * KD].unsqueeze(2).broadcast_to(
                    [P, KD, NS]), ALU.add).then_inc(ys_ok, 1)

            def gated(k, j):
                if not isinstance(k, int) or k > 1:
                    dve.wait_ge(tap_prod, TAPS_ACT * (k - 1))
                dve.tensor_copy(tap_now[:, j, :], taps[:, :].rearrange("p (w k) -> p k w", k=KD)[:, ds(k, 1), :].rearrange(
                    "p a w -> p (a w)")).then_inc(g_ok, 1)
                dve.wait_ge(act_fn, C["fn"] + k + 1)
                dve.wait_ge(evac, t0 + 2 * k + 2)
                dve.tensor_tensor(g_pad[:, j, PAD:PAD + TP], s_up[:, 0:TP], s_act[:, 0:TP], ALU.mult).then_inc(g_ok, 1)
                dve.tensor_tensor(g_last[:, ds(k, 1), :].rearrange("p a t -> p (a t)"), s_up[:, TP - PAD:T],
                                  s_act[:, TP - PAD:T], ALU.mult).then_inc(g_ok, 1)

            def own_taps(k, j, ws):
                for w in ws:
                    acc = (tap_own[:, j, :], s_prod[:, 0:TP])[w % 2]
                    src = g_pad[:, j, w:w + TP]
                    tap = tap_now[:, j, w:w + 1]
                    if w == 0:
                        if not isinstance(k, int) or k > 1:
                            dve.wait_ge(yp_ok, k - 1)
                        dve.wait_ge(g_ok, 3 * k + 2)
                        ins = dve.tensor_scalar(acc, src, tap, gains[:, ds(8 * KD + k, 1)], ALU.mult, ALU.add)
                    elif w == 1:
                        if not isinstance(k, int) or k:
                            dve.wait_ge(y_ok, k)
                        ins = dve.tensor_scalar(acc, src, tap, None, ALU.mult)
                    else:
                        dve.wait_ge(tap_ok, TAPS_DVE * k + w - 1)
                        ins = dve.scalar_tensor_tensor(acc, src, tap, acc, ALU.mult, ALU.add)
                    ins.then_inc(tap_ok, 1)

            def finish(k, j):
                yk = y[:, ds(k, 1), :].rearrange("p a t -> p (a t)")
                dve.wait_ge(tap_ok, TAPS_DVE * k + TAPS_DVE)
                dve.tensor_tensor(tap_own[:, j, :], tap_own[:, j, :], s_prod[:, 0:TP], ALU.add).then_inc(y_ok, 1)
                dve.wait_ge(g_ok, 3 * k + 3)
                dve.wait_ge(ys_ok, 2)
                dve.scalar_tensor_tensor(yk[:, TP:T], g_last[:, ds(k, 1), PAD:].rearrange("p a t -> p (a t)"),
                                         tap_now[:, j, PAD:TAPS], yk[:, TP:T], ALU.mult, ALU.add).then_inc(ys_ok, 1)

            def placed(k, j):
                dve.wait_ge(yp_ok, k + 1)
                dve.tensor_copy(y[:, ds(k, 1), 0:TP].rearrange("p a t -> p (a t)"), tap_sum[:, j, :]).then_inc(yk_ok, 1)

            CUT = 6

            def step(k, j, more):
                scaled(dve, s_up[:, :], 0, n0 + 2 * k)
                if more:
                    split_lo(dve, n0 + 2 * k + 2, 0)
                own_taps(k - 1, 1 - j, range(CUT))
                scaled(dve, s_gate[:, :], 1, n0 + 2 * k + 1)
                if more:
                    split_lo(dve, n0 + 2 * k + 3, 1)
                gated(k, j)
                if not isinstance(k, int) or k > 1:
                    placed(k - 2, j)
                own_taps(k - 1, 1 - j, range(CUT, TAPS_DVE))
                finish(k - 1, 1 - j)

            scaled(dve, s_up[:, :], 0, n0)
            split_lo(dve, n0 + 2, 0)
            scaled(dve, s_gate[:, :], 1, n0 + 1)
            split_lo(dve, n0 + 3, 1)
            gated(0, 0)
            state()
            state_sum()
            step(1, 1, True)
            with dve.Fori(1, KD // 2 - 1) as half:
                for j in range(2):
                    step(2 * half + j, j, True)
            step(KD - 2, 0, True)
            step(KD - 1, 1, False)
            own_taps(KD - 1, 1, range(TAPS_DVE))
            finish(KD - 1, 1)
            dve.wait_ge(ys_ok, KD + 2)
            dve.wait_ge(ysum_ok, 1)
            dve.tensor_reduce(sumsq[:, TP:T], y[:, :, TP:T].rearrange("p k b -> p b k"), AX.X, ALU.add).then_inc(ys_ok, 1)
            placed(KD - 2, 0)
            placed(KD - 1, 1)
            for k in range(KD):
                dve.wait_ge(mean_ok, 1)
                dve.wait_ge(yk_ok, KD)
                dve.tensor_tensor(y[:, k, :], y[:, k, :], log_ms[:, :], ALU.subtract).then_inc(yc_ok, 1)
            dve.wait_ge(var_ok, 2)
            for k in range(KD):
                dve.wait_ge(ysq_ok, k + 1)
                dve.tensor_tensor(y[:, k, :], y[:, k, :], s_up[:, :], ALU.mult).then_inc(yn_ok, 1)
                if k:
                    conv_lo(dve, k - 1)
            conv_lo(dve, KD - 1)

        def conv_lo(dve, k):
            dve.wait_ge(c_hi_ok, k + 1)
            dve.tensor_tensor(c_lo[:, k, :], y[:, k, :], c_hi[:, k, :].bitcast(F32), ALU.subtract).then_inc(c_lo_ok, 1)

        def conv_pool(pool):
            pool.wait_ge(state_ok, 3)
            pool.tensor_tensor(st[:, :, :, :], st[:, :, :, :],
                               taps[:, 0:PAD * KD].rearrange("p (w k) -> p k w", k=KD).unsqueeze(2).broadcast_to(
                                   [P, KD, NS, PAD]), ALU.mult).then_inc(st_prod, 1)
            pool.wait_ge(stat_mm, C["norm"] + 1)

            def tile(k, j):
                ring = lambda c: tap_prods[:, (TAPS_ACT * j + c) % RING, :]
                for c in range(1, TAPS_ACT):
                    pool.wait_ge(tap_prod, TAPS_ACT * k + c + 1)
                    if c == 1:
                        if not isinstance(k, int) or k > 1:
                            pool.wait_ge(yk_ok, k - 1)
                            pool.wait_ge(ysum_ok, k)
                        pool.tensor_tensor(tap_sum[:, j, :], ring(0), ring(1), ALU.add).then_inc(tap_add, 1)
                    else:
                        pool.wait_ge(tap_add, (TAPS_ACT - 1) * k + c - 1)
                        pool.tensor_tensor(tap_sum[:, j, :], tap_sum[:, j, :], ring(c), ALU.add).then_inc(tap_add, 1)
                pool.wait_ge(y_ok, k + 1)
                pool.wait_ge(tap_add, (TAPS_ACT - 1) * (k + 1))
                pool.tensor_tensor(tap_sum[:, j, :], tap_sum[:, j, :], tap_own[:, j, :], ALU.add).then_inc(yp_ok, 1)
                pool.wait_ge(yp_ok, k + 1)
                if isinstance(k, int) and k == 0:
                    pool.tensor_copy(sumsq[:, 0:TP], tap_sum[:, 0, :]).then_inc(ysum_ok, 1)
                else:
                    pool.wait_ge(ysum_ok, k)
                    pool.tensor_tensor(sumsq[:, 0:TP], sumsq[:, 0:TP], tap_sum[:, j, :], ALU.add).then_inc(ysum_ok, 1)

            tile(0, 0)
            tile(1, 1)
            with pool.Fori(1, KD // 2) as half:
                for j in range(2):
                    tile(2 * half + j, j)
            pool.wait_ge(ln_mm, 1)
            for k in range(KD):
                pool.wait_ge(ysq_ok, k + 1)
                if k == 0:
                    pool.tensor_copy(sumsq[:, :], square[:, 0, :]).then_inc(ysum_ok, 1)
                else:
                    pool.wait_ge(ysum_ok, KD + k)
                    pool.tensor_tensor(sumsq[:, :], sumsq[:, :], square[:, k % 2, :], ALU.add).then_inc(ysum_ok, 1)

        y_mm = sem("y_mm")
        y_tok = sem("y_tok")
        y_out = [sem("y_out0"), sem("y_out1")]

        def ple_sp(sp, a, layer):
            n0 = a["slab"]
            for g in range(2):
                src = io["ple_w_proj"][layer].rearrange("(k p) f -> p k f", p=P)[:, :, g * 4 * P:(g + 1) * 4 * P]
                sp.wait_ge(slab_lo, n0 + g - 1)
                sp.dma_start(w_raw[:, g, 0:KP * 4 * P].rearrange("p (k c) -> p k c", k=KP), src).then_inc(slab_in[g], 16)
            with sp.Fori(0, KD // 2) as half:
                for j in range(2):
                    load_slab(sp, n0 + 2 + 2 * half + j, j, slab_src(io["ple_w_gate"][layer], 2 * half + j), KD)
            if layer == 0:
                load_p(sp, 1)
            else:
                for m in range(KD):
                    sp.wait_ge(y_tok, 2 * m + 2)
                    sp.dma_start(io["y_prompt"][0].rearrange("(n p) f -> p n f", p=P)[:, :, m * P:(m + 1) * P],
                                 out_tok[:, m % 2, :, :]).then_inc(y_out[m % 2], 16)
                sp.dma_start(io["y_sample"].rearrange("b a f -> (b a) f"), outs_tok[:, :]).then_inc(y_out[0], 16)

        def ple_pe(pe, a, layer):
            n0, t0 = a["slab"], a["tile"]
            pe.wait_ge(p_in, 32 * (layer + 1))
            for k in range(KP):
                for n in range(NT):
                    pe.transpose(ps[:, 2 + k, 0, n * P:(n + 1) * P], p_tok[:, n, k * P:(k + 1) * P], ident[:, :])
                pe.transpose(ps[:, 2 + k, 1, 0:NS], ps_tok[:, k * P:(k + 1) * P], ident[0:NS, 0:NS]).then_inc(p_t, 1)
            for m in range(KD):
                g, q = divmod(m, 4)
                if q == 0:
                    pe.wait_ge(slab_lo, n0 + g + 1)
                if m == 0:
                    pe.wait_ge(p_lo_ok, 2 * KP * (layer + 1))
                pe.wait_ge(evac, t0 + m - 1)
                for k in range(KP):
                    w = slice((k * 4 + q) * P, (k * 4 + q + 1) * P)
                    for n, (wt, mv) in enumerate(((w_hi, p_hi), (w_hi, p_lo), (w_lo, p_hi))):
                        for b in range(2):
                            ins = pe.matmul(ps[:, m % 2, b, 0:HALF], wt[:, g, w], mv[:, k, b * HALF:(b + 1) * HALF],
                                            start=k == 0 and n == 0, stop=k == KP - 1 and n == 2)
                ins.then_inc(slab_used if q == 3 else pp_mm, 1)

            def gate(m, s, wait_h=False):
                pe.wait_ge(slab_lo, n0 + 3 + m)
                pe.wait_ge(evac, t0 + KD + m - 1)
                wait_k = (lambda k: pe.wait_ge(h_lo_ok, at["down2", layer]["xt"] + k + 1)) if wait_h else None
                products(pe, slot(s), s, 0, range(KD), h_hi, h_lo, 0, True, True, wait_k).then_inc(slab_used, 1)

            def turned(m):
                pe.wait_ge(x_new, KD + m + 1)
                pe.wait_ge(y_tok, 2 * m - 2) if m > 1 else None
                for n in range(NT):
                    pe.transpose(ps[:, 2 + m % 2, 0, n * P:(n + 1) * P], x[:, m, n * P:(n + 1) * P], ident[:, :])
                pe.transpose(ps[0:NS, 2 + m % 2, 1, 0:P], x[:, m, TP:T], ident[:, :]).then_inc(y_mm, 1)

            gate(0, 0, True)
            stat_pe(pe, dict(a, xt=at["down2", layer]["xt"] + KD))
            gate(1, 1)
            if layer == 0:
                with pe.Fori(1, KD // 2) as half:
                    gate(2 * half, 0)
                    gate(2 * half + 1, 1)
            else:
                pe.wait_ge(rms_ok, a["norm"] + 1)
                for m in range(2, KD):
                    gate(m, m % 2)
                    if m >= 4:
                        turned(m - 4)
                for m in range(4, KD):
                    turned(m)

        def ple_act(act, a, layer, prev):
            n0 = a["slab"]
            split_hi(act, n0, n0 // 2, 0)
            for k in range(KP):
                act.wait_ge(p_t, KP * layer + k + 1)
                act.activation(p_hi[:, k, 0:TP], ps[:, 2 + k, 0, :], ACT.Copy).then_inc(p_hi_ok, 1)
                act.activation(p_hi[:, k, TP:T], ps[:, 2 + k, 1, 0:NS], ACT.Copy).then_inc(p_hi_ok, 1)
            prev(0)
            split_hi(act, n0 + 1, n0 // 2, 1)
            prev(1)
            split_hi(act, n0 + 2, n0 // 2 + 1, 0)
            split_hi(act, n0 + 3, n0 // 2 + 1, 1)
            stat_act(act, a)

            def sigmoid(m):
                act.wait_ge(evac, a["tile"] + KD + m + 1)
                act.activation(s_act[:, :], s_gate[:, :], ACT.Sigmoid).then_inc(act_fn, 1)

            def finish(m):
                if layer == 0:
                    act.wait_ge(x_new, m + 1)
                    act.wait_ge(acc_ok, a["xt"] + m - 1)
                    act.activation(square[:, m % 2, :], x[:, m, :],
                                   ACT.Square).then_inc(sq_ok, 1)
                else:
                    act.wait_ge(y_mm, m + 1)
                    if m >= 2:
                        act.wait_ge(y_out[m % 2], 16 * (m // 2))
                    act.activation(out_tok[:, m % 2, :, :].rearrange("p n f -> p (n f)"), ps[:, 2 + m % 2, 0, :],
                                   ACT.Copy).then_inc(y_tok, 1)
                    act.activation(outs_tok[:, m * P:(m + 1) * P], ps[0:NS, 2 + m % 2, 1, 0:P], ACT.Copy).then_inc(y_tok, 1)

            for m in range(KD):
                if m < KD - 2:
                    split_hi(act, n0 + 4 + m, n0 // 2 + 2 + m // 2, m % 2)
                sigmoid(m)
                if layer == 0:
                    finish(m)
                elif m >= 4:
                    finish(m - 4)
            if layer == 1:
                for m in range(4, KD):
                    finish(m)

        def ple_dve(dve, a, layer, prev_evac, prev_lo):
            n0, t0 = a["slab"], a["tile"]
            prev_evac(0)
            prev_evac(1)
            split_lo(dve, n0, 0)
            for k in range(KP):
                for c, (lo, hi, src) in enumerate(((p_lo[:, k, 0:TP], p_hi[:, k, 0:TP], ps[:, 2 + k, 0, :]),
                                                   (p_lo[:, k, TP:T], p_hi[:, k, TP:T], ps[:, 2 + k, 1, 0:NS]))):
                    dve.wait_ge(p_hi_ok, 2 * (KP * layer + k) + c + 1)
                    dve.tensor_tensor(lo, src, hi.bitcast(F32), ALU.subtract).then_inc(p_lo_ok, 1)
            split_lo(dve, n0 + 1, 1)
            prev_lo(0)
            prev_lo(1)
            for m in range(KD):
                g, q = divmod(m, 4)
                dve.wait_ge(slab_used, n0 + g + 1) if q == 3 else dve.wait_ge(pp_mm, 6 * layer + 3 * g + q + 1)
                dve.tensor_copy(halves(pp[:, m, :]), slot(m % 2)).then_inc(evac, 1)
                if q == 3:
                    split_lo(dve, n0 + 2 + g, g)
            dve.wait_ge(rms_ok, a["norm"] + 1)
            for m in range(KD):
                scaled(dve, s_gate[:, :], m % 2, n0 + 2 + m)
                if m < KD - 2:
                    split_lo(dve, n0 + 4 + m, m % 2)
                dve.wait_ge(act_fn, a["fn"] + m + 1)
                dve.tensor_tensor(s_prod[:, :], s_act[:, :], pp[:, m, :], ALU.mult).then_inc(prod_x, 1)
                dve.wait_ge(prod_x, KD * layer + m + 1)
                dve.tensor_tensor(x[:, m, :], x[:, m, :], s_prod[:, :], ALU.add).then_inc(x_new, 1)

        def ple_pool(pool, a):
            for m in range(KD):
                x_add_pool(pool, a, m, m % 2, m == 0)

        def after_ple(a):
            def act_part(act):
                def run_(j):
                    if j == 0:
                        act.wait_ge(slab_used, a["slab"] + 2 + KD)
                        for m in range(KD):
                            act.activation(h_hi[:, m, :], x[:, m, :], ACT.Copy,
                                           scale=gain_col(1, 0, m)).then_inc(h_hi_ok, 1)
                return run_

            def dve_lo(dve):
                return lambda j: [x_post_dve(dve, a, 1, 0, m) for m in range(KD)] if j == 0 else None
            return act_part, (lambda dve: nothing), dve_lo

        block = ctx.enter_context(nc.Block())
        LAYERS = range(2)

        @block.sync
        def _(sp):
            load_sp(sp)
            for layer in LAYERS:
                up_sp(sp, at["up1", layer], layer, io["ffn1_wg"], io["ffn1_wu"])
                to_x_sp(sp, at["down1", layer], 2, io["ffn1_wd"][layer])
                if layer == 0:
                    attn_sp(sp)
                    to_x_sp(sp, at["mixout", 0], 1, io["attn_w_o"][0])
                else:
                    conv_sp(sp)
                    to_x_sp(sp, at["mixout", 1], 1, io["conv_w_out"][0])
                up_sp(sp, at["up2", layer], layer, io["ffn2_wg"], io["ffn2_wu"])
                to_x_sp(sp, at["down2", layer], 2, io["ffn2_wd"][layer])
                ple_sp(sp, at["ple", layer], layer)
            sp.wait_ge(k_out, 32 * NP)
            sp.wait_ge(v_out, 32 * NP)
            sp.wait_ge(conv_out, 96)
            sp.wait_ge(y_out[0], 16 * (KD // 2 + 1))
            sp.wait_ge(y_out[1], 16 * (KD // 2))

        @block.gpsimd
        def _(pool):
            load_pool(pool)
            add_squares_pool(pool, L)
            for layer in LAYERS:
                add_squares_pool(pool, at["down1", layer])
                (attn_pool, conv_pool)[layer](pool)
                add_squares_pool(pool, at["mixout", layer])
                add_squares_pool(pool, at["down2", layer])
                if layer == 0:
                    ple_pool(pool, at["ple", 0])

        after = {}
        for layer in LAYERS:
            after["up1", layer] = after_up(at["up1", layer])
            after["up2", layer] = after_up(at["up2", layer])
            after["down1", layer] = after_to_x(at["down1", layer], 2, layer, 1, 0.5)
            after["mixout", layer] = after_to_x(at["mixout", layer], 1, layer, 2, 1.0)
            after["down2", layer] = after_to_x(at["down2", layer], 2, layer, 3, 0.5)
        before_up1 = (after_load(), after_ple(at["ple", 0]))

        @block.scalar
        def _(act):
            load_act(act)
            for layer in LAYERS:
                up_act(act, at["up1", layer], before_up1[layer][0](act))
                to_x_act(act, at["down1", layer], 2, layer, 1, after["up1", layer][0](act))
                (attn_act, conv_act)[layer](act, after["down1", layer][0](act))
                if layer == 0:
                    act.wait_ge(k_out, 32 * NP)
                    act.wait_ge(v_out, 32 * NP)
                to_x_act(act, at["mixout", layer], 1, layer, 2, nothing)
                if layer == 1:
                    act.wait_ge(conv_out, 96)
                up_act(act, at["up2", layer], after["mixout", layer][0](act))
                to_x_act(act, at["down2", layer], 2, layer, 3, after["up2", layer][0](act))
                ple_act(act, at["ple", layer], layer, after["down2", layer][0](act))

        @block.vector
        def _(dve):
            load_dve(dve)
            for layer in LAYERS:
                up_dve(dve, at["up1", layer], before_up1[layer][1](dve), before_up1[layer][2](dve))
                to_x_dve(dve, at["down1", layer], 2, layer, 1, 0.5, after["up1", layer][1](dve), after["up1", layer][2](dve))
                (attn_dve, conv_dve)[layer](dve, after["down1", layer][1](dve), after["down1", layer][2](dve))
                to_x_dve(dve, at["mixout", layer], 1, layer, 2, 1.0, nothing, nothing)
                up_dve(dve, at["up2", layer], after["mixout", layer][1](dve), after["mixout", layer][2](dve))
                to_x_dve(dve, at["down2", layer], 2, layer, 3, 0.5, after["up2", layer][1](dve), after["up2", layer][2](dve))
                ple_dve(dve, at["ple", layer], layer, after["down2", layer][1](dve), after["down2", layer][2](dve))

        @block.tensor
        def _(pe):
            load_pe(pe)
            for layer in LAYERS:
                U1, U2 = at["up1", layer], at["up2", layer]
                up_pe(pe, U1)
                to_x_pe(pe, at["down1", layer], 2, a_hi, a_lo, a_lo_ok, U1["hid"], KF)
                (attn_pe, conv_pe)[layer](pe)
                if layer == 0:
                    to_x_pe(pe, at["mixout", 0], 1, o_hi, o_lo, os_ok, 0, 3 * NP)
                else:
                    to_x_pe(pe, at["mixout", 1], 1, c_hi, c_lo, c_lo_ok, 0, KD)
                up_pe(pe, U2)
                to_x_pe(pe, at["down2", layer], 2, a_hi, a_lo, a_lo_ok, U2["hid"], KF)
                ple_pe(pe, at["ple", layer], layer)


_INS = ("x_prompt", "x_sample", "cache_k", "cache_v", "state_conv", "page_table", "p_prompt", "p_sample",
        "norm_ffn1", "ffn1_wg", "ffn1_wu", "ffn1_wd", "norm_mix", "attn_w_qkv", "attn_q_norm", "attn_k_norm",
        "attn_logit_bias", "attn_w_o", "conv_w_in", "conv_w_dw", "conv_b_dw", "conv_ln_g", "conv_ln_b",
        "conv_w_out", "norm_ffn2", "ffn2_wg", "ffn2_wu", "ffn2_wd", "norm_ple", "ple_w_gate", "ple_w_proj")
_OUTS = (("y_prompt", (1, 512, 1024)), ("y_sample", (8, 1, 1024)),
         ("new_k_prompt", (1, 1, 512, 16, 64)), ("new_v_prompt", (1, 1, 512, 16, 64)),
         ("new_k_sample", (1, 8, 1, 16, 64)), ("new_v_sample", (1, 8, 1, 16, 64)),
         ("new_conv_prompt", (1, 1, 30, 1024)), ("new_conv_sample", (1, 8, 30, 1024)))


def kernel(**inputs):
    import numpy as _np
    import concourse.bacc as _bacc
    from concourse import mybir as _mybir
    from concourse.bass_utils import run_bass_kernel_spmd as _run

    nc = _bacc.Bacc("TRN2", target_bir_lowering=False, num_devices=1)
    arrays, io = {}, {}
    for name in _INS:
        a = _np.ascontiguousarray(inputs[name])
        arrays[f"in_{name}"] = a
        io[name] = nc.dram_tensor(f"in_{name}", a.shape, _mybir.dt.from_np(a.dtype), kind="ExternalInput").ap()
    for name, shape in _OUTS:
        io[name] = nc.dram_tensor(f"out_{name}", shape, _mybir.dt.float32, kind="ExternalOutput").ap()
    build(nc, io)
    r = _run(nc, [arrays], core_ids=[0])
    return tuple(r.results[0][f"out_{name}"] for name, _ in _OUTS)
```

```python
from contextlib import ExitStack

import concourse.bass as bass
from concourse import mybir

F32 = mybir.dt.float32
F32R = mybir.dt.float32r
I32 = mybir.dt.int32
ACT = mybir.ActivationFunctionType
ALU = mybir.AluOpType
AX = mybir.AxisListType
ds = bass.ds

P = 128
D = 1024
KD = D // P
FF = 2816
KF = FF // P
KH = KF // 2
TP = 512
NT = TP // P
NS = 8
T = TP + NS
HALF = T // 2
NH = 16
HD = 64
NP = KD
PG = 4
TAPS = 31
PAD = TAPS - 1
TAPS_DVE, TAPS_ACT, TAPS_PE = 16, 12, 3
LAST_DVE, LAST_ACT, LAST_PE = 13, 8, 10
RING = 4
DP = 256
KP = DP // P
EPS = 1e-6
LN_EPS = 1e-5
SLAB = KH * P
LOG_EXP = "natural_log_exp_and_others"
NORMS = ("norm_ffn1", "norm_mix", "norm_ffn2", "norm_ple")
VECS = 11 * KD

def build(nc, io):
    ctx = ExitStack()
    with ctx:
        def sb(name, shape, dt=F32):
            return ctx.enter_context(nc.sbuf_tensor(name, shape, dt))

        def sem(name):
            return ctx.enter_context(nc.semaphore(name))

        x = sb("x", [P, KD, T])
        h_hi = sb("h_hi", [P, KD, T], F32R)
        h_lo = sb("h_lo", [P, KD, T], F32R)
        w_raw = sb("w_raw", [P, 2, SLAB])
        w_hi = sb("w_hi", [P, 2, SLAB], F32R)
        w_lo = sb("w_lo", [P, 2, SLAB], F32R)
        square = sb("square", [P, 2, T])
        sumsq = sb("sumsq", [P, T])
        log_ms = sb("log_ms", [P, T])
        rms = sb("rms", [P, T])
        s_gate = sb("s_gate", [P, T])
        s_up = sb("s_up", [P, T])
        s_act = sb("s_act", [P, T])
        s_prod = sb("s_prod", [P, T])
        p_tok = sb("p_tok", [P, NT, DP])
        ps_tok = sb("ps_tok", [NS, DP])
        ident = sb("ident", [P, P])
        ones = sb("ones", [P, P])
        head_ones = sb("head_ones", [P, P])
        from_here = sb("from_here", [P, P])
        not_before = sb("not_before", [P, P])
        gains = sb("gains", [P, VECS])
        taps = sb("taps", [P, TAPS * KD])
        qk_gain = sb("qk_gain", [P, 2])
        bias = sb("bias", [P, NH])
        eps = sb("eps", [P, 2])
        pages = sb("pages", [1, NS * PG], I32)

        def phase_memory(*specs):
            with ExitStack() as stack:
                return [stack.enter_context(nc.sbuf_tensor(n, s, d)) for n, s, d in specs]

        x_tok, xs_tok, vec_rows, tap_rows = phase_memory(
            ("x_tok", [P, NT, D], F32), ("xs_tok", [NS, D], F32), ("vec_rows", [VECS, P], F32),
            ("tap_rows", [TAPS * KD // 2, 2, P], F32))
        a_hi, a_lo = phase_memory(("a_hi", [P, KF, T], F32R), ("a_lo", [P, KF, T], F32R))
        (o_hi, o_lo, k_f, v_tok, l_b, sp_a, sp_1, run, a_b, kc, vc,
         zs, ls, sps, runs) = phase_memory(
            ("o_hi", [P, KD, T], F32R), ("o_lo", [P, KD, T], F32R), ("k_f", [P, T], F32),
            ("v_tok", [P, NT, P], F32),
            ("l_b", [P, 2, 2, TP], F32), ("sp_a", [P, 2, TP], F32), ("sp_1", [P, 2, 3 * P], F32), ("run", [P, 2, TP], F32),
            ("a_b", [P, 2 * (TP + 6 * P)], F32), ("kc", [P, PG, D], F32), ("vc", [P, PG, D], F32),
            ("zs", [P, PG, 2 * NS], F32), ("ls", [P, PG, 2 * NS], F32),
            ("sps", [P, PG, 2 * NS], F32), ("runs", [P, PG, 2 * NS], F32))
        q_all, = phase_memory(("q_all", [P, KD, T], F32))
        g_pad, tap_now, tap_prods, tap_sum, tap_own, diag0, diag1, g_last, st_rows, st, y, c_hi, c_lo, cv_tok = phase_memory(
            ("g_pad", [P, 2, PAD + TP], F32), ("tap_now", [P, 2, TAPS], F32), ("tap_prods", [P, RING, TP], F32),
            ("tap_sum", [P, 2, TP], F32), ("tap_own", [P, 2, TP], F32), ("diag0", [P, TAPS_PE, P], F32),
            ("diag1", [P, LAST_PE, P], F32), ("g_last", [P, KD, PAD + NS], F32), ("st_rows", [4 * PAD, 2, D], F32),
            ("st", [P, KD, NS, PAD], F32), ("y", [P, KD, T], F32), ("c_hi", [P, KD, T], F32R),
            ("c_lo", [P, KD, T], F32R), ("cv_tok", [PAD + NS, D], F32))
        p_hi, p_lo, pp, out_tok, outs_tok = phase_memory(
            ("p_hi", [P, KP, T], F32R), ("p_lo", [P, KP, T], F32R), ("pp", [P, KD, T], F32),
            ("out_tok", [P, 2, NT, P], F32), ("outs_tok", [NS, D], F32))

        ps = ctx.enter_context(nc.psum_tensor("ps", [P, 4, 2, 512], F32))

        q_f = sumsq
        k_raw, v_f, qk_r = s_up, s_act, s_prod
        k_tok = log_ms[:, 0:TP].rearrange("p (n f) -> p n f", n=NT)
        kvs_tok = square[0:NS, 1, 0:2 * P].rearrange("p (c f) -> p c f", c=2)
        q_bc = run[:, :, :].rearrange("p e t -> p (e t)")
        q_diag = l_b[:, 1, :, :].rearrange("p e t -> p (e t)")

        def halves(ap):
            return ap.rearrange("p (b n) -> p b n", b=2)

        def slot(s):
            return ps[:, s, :, 0:HALF]

        def flat(s, b=0):
            return ps[:, s, b, :]

        slab_in = [sem("slab_in0"), sem("slab_in1")]
        slab_hi = sem("slab_hi")
        slab_lo = sem("slab_lo")
        slab_used = sem("slab_used")
        evac = sem("evac")
        h_hi_ok = sem("h_hi_ok")
        h_lo_ok = sem("h_lo_ok")
        sq_ok = sem("sq_ok")
        acc_ok = sem("acc_ok")
        stat_mm = sem("stat_mm")
        log_ok = sem("log_ok")
        rms_ok = sem("rms_ok")
        act_fn = sem("act_fn")
        prod_ok = sem("prod_ok")
        a_hi_ok = sem("a_hi_ok")
        a_lo_ok = sem("a_lo_ok")
        const_ok = sem("const_ok")
        const_set = sem("const_set")
        first_in = [sem(f"first_in{n}") for n in range(4)]
        load_t = sem("load_t")
        vec_t = sem("vec_t")
        vec_ok = sem("vec_ok")
        p_in = sem("p_in")
        p_t = sem("p_t")
        p_hi_ok = sem("p_hi_ok")
        p_lo_ok = sem("p_lo_ok")
        pp_mm = sem("pp_mm")
        prod_x = sem("prod_x")
        x_new = sem("x_new")

        at = {}
        slab = tile = norm = hid = xt = fn = 0
        for layer in range(2):
            for name in (("load",) if layer == 0 else ()) + ("up1", "down1", "mix", "mixout", "up2", "down2", "ple"):
                at[name, layer] = dict(slab=slab, tile=tile, norm=norm, hid=hid, xt=xt, fn=fn)
                if name == "load":
                    tile += KD
                    xt += KD
                if name[:2] == "up":
                    slab += 2 * KF
                    tile += 2 * KF
                    fn += KF
                    hid += KF
                    norm += 1
                if name[:4] == "down":
                    slab += 2 * KD
                    tile += KD
                    xt += KD
                if name == "mix":
                    n = 3 * NP if layer == 0 else 2 * KD
                    slab += n
                    tile += n
                    fn += 0 if layer == 0 else KD
                    norm += 1
                if name == "mixout":
                    slab += KD
                    tile += KD
                    xt += KD
                if name == "ple":
                    slab += 2 + KD
                    tile += 2 * KD
                    fn += KD
                    xt += KD if layer == 0 else 0
                    norm += 1

        def gain_col(layer, which, m):
            return gains[:, ds((which * 2 + layer) * KD + m, 1)]

        def load_slab(sp, n, j, src, kt):
            sp.wait_ge(slab_lo, n - 1)
            dst = w_raw[:, j, 0:kt * P].rearrange("p (k c) -> p k c", k=kt)
            sp.dma_start(dst, src).then_inc(slab_in[j], 16)

        def split_hi(act, n, half, j, cols=KD * P):
            act.wait_ge(slab_in[j], 16 * half + 16)
            act.wait_ge(slab_used, n - 1)
            act.activation(w_hi[:, j, 0:cols], w_raw[:, j, 0:cols], ACT.Copy).then_inc(slab_hi, 1)

        def split_lo(dve, n, j, cols=KD * P):
            dve.wait_ge(slab_hi, n + 1)
            dve.tensor_tensor(w_lo[:, j, 0:cols], w_raw[:, j, 0:cols], w_hi[:, j, 0:cols].bitcast(F32),
                              ALU.subtract).then_inc(slab_lo, 1)

        def products(pe, out, j, w0, kts, hi, lo, k0, first, last, wait_k=None, token_halves=(0, 1)):
            for k in kts:
                if wait_k is not None:
                    wait_k(k)
                w = slice(w0 + k * P, w0 + (k + 1) * P)
                for n, (a, b) in enumerate(((w_hi, hi), (w_hi, lo), (w_lo, hi))):
                    for b_ in token_halves:
                        ins = pe.matmul(out[:, b_, :], a[:, j, w], b[:, k0 + k, b_ * HALF:(b_ + 1) * HALF],
                                        start=(first and k == kts[0] and n == 0),
                                        stop=(last and k == kts[-1] and n == 2))
            return ins

        def x_post_act(act, at_, layer, which, m, m2):
            xm = x[:, ds(m, 1), :].rearrange("p a t -> p (a t)")
            if at_["xt"] or m > 1:
                act.wait_ge(acc_ok, at_["xt"] + m - 1)
            act.wait_ge(evac, at_["tile"] + m + 1)
            act.activation(h_hi[:, ds(m, 1), :].rearrange("p a t -> p (a t)"), xm, ACT.Copy,
                           scale=gain_col(layer, which, m)).then_inc(h_hi_ok, 1)
            act.activation(square[:, m2, :], xm, ACT.Square).then_inc(sq_ok, 1)

        def x_post_dve(dve, at_, layer, which, m):
            dve.wait_ge(h_hi_ok, at_["xt"] + m + 1)
            dve.scalar_tensor_tensor(h_lo[:, ds(m, 1), :].rearrange("p a t -> p (a t)"),
                                     x[:, ds(m, 1), :].rearrange("p a t -> p (a t)"), gain_col(layer, which, m),
                                     h_hi[:, ds(m, 1), :].rearrange("p a t -> p (a t)").bitcast(F32),
                                     ALU.mult, ALU.subtract).then_inc(h_lo_ok, 1)

        def x_add_pool(pool, at_, m, m2, first=False):
            pool.wait_ge(sq_ok, at_["xt"] + m + 1)
            if first:
                if at_["norm"]:
                    pool.wait_ge(stat_mm, at_["norm"])
                pool.tensor_copy(sumsq[:, :], square[:, m2, :]).then_inc(acc_ok, 1)
            else:
                pool.wait_ge(acc_ok, at_["xt"] + m)
                pool.tensor_tensor(sumsq[:, :], sumsq[:, :], square[:, m2, :], ALU.add).then_inc(acc_ok, 1)

        def stat_pe(pe, a):
            pe.wait_ge(acc_ok, a["xt"])
            for b in range(2):
                ins = pe.matmul(ps[:, 3, b, 0:HALF], ones[:, :], sumsq[:, b * HALF:(b + 1) * HALF],
                                start=True, stop=True)
            ins.then_inc(stat_mm, 1)

        def stat_act(act, a):
            act.preload_act_table_set(LOG_EXP)
            act.wait_ge(stat_mm, a["norm"] + 1)
            act.activation(halves(log_ms[:, :]), slot(3), ACT.Ln, scale=1.0 / D, bias=eps[:, 0:1]).then_inc(log_ok, 1)
            act.wait_ge(log_ok, a["norm"] + 1)
            act.activation(rms[:, :], log_ms[:, :], ACT.Exp, scale=-0.5).then_inc(rms_ok, 1)

        def scaled(dve, out, s, n):
            dve.wait_ge(slab_used, n + 1)
            dve.tensor_tensor(halves(out), slot(s), halves(rms[:, :]), ALU.mult).then_inc(evac, 1)

        def add_to_x(dve, s, n, m, factor):
            dve.wait_ge(slab_used, n + 1)
            xm = x[:, ds(m, 1), :].rearrange("p a (b n) -> p (a b) n", b=2)
            dve.scalar_tensor_tensor(xm, slot(s), factor, xm, ALU.mult, ALU.add).then_inc(evac, 1)

        def slab_src(w, m, k0=0, kt=KD):
            return w.rearrange("(k p) f -> p k f", p=P)[:, k0:k0 + kt, ds(m * P, P)]

        def up_sp(sp, a, layer, wg, wu):
            n0 = a["slab"]
            with sp.Fori(1 if n0 == 0 else 0, KF) as f:
                for j, w in ((0, wg), (1, wu)):
                    load_slab(sp, n0 + 2 * f + j, j, slab_src(w[layer], f), KD)

        def silu_act(act, a, f):
            act.wait_ge(evac, a["tile"] + 2 * f + 1)
            act.activation(s_act[:, :], s_gate[:, :], ACT.Silu).then_inc(act_fn, 1)

        def hidden_hi_act(act, a, f):
            act.wait_ge(prod_ok, a["hid"] + f + 1)
            act.activation(a_hi[:, ds(f, 1), :].rearrange("p a t -> p (a t)"), s_prod[:, :],
                           ACT.Copy).then_inc(a_hi_ok, 1)

        def hidden_dve(dve, a, f):
            dve.wait_ge(act_fn, a["fn"] + f + 1)
            dve.wait_ge(evac, a["tile"] + 2 * f + 2)
            dve.tensor_tensor(s_prod[:, :], s_act[:, :], s_up[:, :], ALU.mult).then_inc(prod_ok, 1)
            dve.wait_ge(a_hi_ok, a["hid"] + f + 1)
            dve.tensor_tensor(a_lo[:, ds(f, 1), :].rearrange("p a t -> p (a t)"), s_prod[:, :],
                              a_hi[:, ds(f, 1), :].rearrange("p a t -> p (a t)").bitcast(F32),
                              ALU.subtract).then_inc(a_lo_ok, 1)

        def up_act(act, a, prev):
            n0 = a["slab"]
            for j in range(2) if prev else ():
                if n0:
                    split_hi(act, n0 + j, n0 // 2, j)
                elif j:
                    act.wait_ge(slab_in[j], 16)
                    act.activation(w_hi[:, j, 0:D], w_raw[:, j, 0:D], ACT.Copy).then_inc(slab_hi, 1)
                prev(j)
            for f in range(1, 2):
                split_hi(act, n0 + 2 * f, n0 // 2 + f, 0)
                stat_act(act, a)
                silu_act(act, a, f - 1)
                split_hi(act, n0 + 2 * f + 1, n0 // 2 + f, 1)
                hidden_hi_act(act, a, f - 1)
            with act.Fori(2, KF) as f:
                split_hi(act, n0 + 2 * f, n0 // 2 + f, 0)
                silu_act(act, a, f - 1)
                split_hi(act, n0 + 2 * f + 1, n0 // 2 + f, 1)
                hidden_hi_act(act, a, f - 1)

        def up_dve(dve, a, prev_evac, prev_lo):
            n0, t0 = a["slab"], a["tile"]
            for j in range(2) if prev_lo else ():
                prev_evac(j)
                if n0 or j:
                    split_lo(dve, n0 + j, j)
                prev_lo(j)

            def step(f, s):
                scaled(dve, s_gate[:, :], s, n0 + 2 * f - 2)
                split_lo(dve, n0 + 2 * f, 0)
                scaled(dve, s_up[:, :], s + 1, n0 + 2 * f - 1)
                split_lo(dve, n0 + 2 * f + 1, 1)
                hidden_dve(dve, a, f - 1)

            dve.wait_ge(rms_ok, a["norm"] + 1)
            step(1, 0)
            with dve.Fori(1, KF // 2) as half:
                f = 2 * half
                step(f, 2)
                step(f + 1, 0)

        def up_pe(pe, a):
            n0, t0 = a["slab"], a["tile"]

            def gate_or_up(f, c, s, wait_h=False, free=None):
                pe.wait_ge(slab_lo, n0 + 2 * f + c + 1)
                pe.wait_ge(evac, t0 + 2 * f + c - 3 if free is None else free)
                wait_k = (lambda k: pe.wait_ge(h_lo_ok, a["xt"] - KD + k + 1)) if wait_h else None
                ins = products(pe, slot(s), c, 0, range(KD), h_hi, h_lo, 0, True, True, wait_k)
                ins.then_inc(slab_used, 1)

            gate_or_up(0, 0, 0, True, t0 - 1)
            pe.wait_ge(evac, t0)
            stat_pe(pe, a)
            gate_or_up(0, 1, 1, False, t0)
            gate_or_up(1, 0, 2, False, t0)
            pe.wait_ge(rms_ok, a["norm"] + 1)
            gate_or_up(1, 1, 3, False, t0)
            with pe.Fori(1, KF // 2) as half:
                f = 2 * half
                gate_or_up(f, 0, 0)
                gate_or_up(f, 1, 1)
                gate_or_up(f + 1, 0, 2)
                gate_or_up(f + 1, 1, 3)

        def to_x_sp(sp, a, spt, w, loaded=0):
            n0 = a["slab"]
            with sp.Fori(loaded // 2, KD * spt // 2) as step:
                m = 2 // spt * step
                for j in range(2):
                    src = slab_src(w, m, j * KH, KH) if spt == 2 else slab_src(w, m + j)
                    load_slab(sp, n0 + spt * m + j, j, src, KH if spt == 2 else KD)

        def to_x_act(act, a, spt, layer, which, prev):
            n0, cols = a["slab"], (KH if spt == 2 else KD) * P
            for j in range(2) if prev else ():
                split_hi(act, n0 + j, n0 // 2, j, cols)
                prev(j)

            def post(m, m2):
                x_post_act(act, a, layer, which, m, m2)

            if spt == 2:
                def step(m, m2):
                    split_hi(act, n0 + 2 * m, n0 // 2 + m, 0, cols)
                    split_hi(act, n0 + 2 * m + 1, n0 // 2 + m, 1, cols)
                    post(m - 1, m2)
                step(1, 0)
                with act.Fori(1, KD // 2) as half:
                    m = 2 * half
                    step(m, 1)
                    step(m + 1, 0)
            else:
                with act.Fori(1, KD // 2) as u:
                    for j in range(2):
                        split_hi(act, n0 + 2 * u + j, n0 // 2 + u, j, cols)
                        post(2 * u + j - 2, j)

        def to_x_dve(dve, a, spt, layer, which, factor, prev_evac, prev_lo):
            n0, cols = a["slab"], (KH if spt == 2 else KD) * P
            for j in range(2) if prev_lo else ():
                prev_evac(j)
                split_lo(dve, n0 + j, j, cols)
                prev_lo(j)
            if spt == 2:
                def step(m, s):
                    split_lo(dve, n0 + 2 * m, 0, cols)
                    add_to_x(dve, s, n0 + 2 * m - 1, m - 1, factor)
                    split_lo(dve, n0 + 2 * m + 1, 1, cols)
                    x_post_dve(dve, a, layer, which, m - 1)
                step(1, 0)
                with dve.Fori(1, KD // 2) as half:
                    m = 2 * half
                    step(m, 1)
                    step(m + 1, 0)
            else:
                with dve.Fori(1, KD // 2) as half:
                    m = 2 * half
                    for j in range(2):
                        add_to_x(dve, j, n0 + m + j - 2, m + j - 2, factor)
                        split_lo(dve, n0 + m + j, j, cols)
                        x_post_dve(dve, a, layer, which, m + j - 2)

        def add_squares_pool(pool, a):
            x_add_pool(pool, a, 0, 0, True)
            x_add_pool(pool, a, 1, 1)
            with pool.Fori(1, KD // 2) as half:
                m = 2 * half
                x_add_pool(pool, a, m, 0)
                x_add_pool(pool, a, m + 1, 1)

        def down_pe(pe, a, hidden):
            n0, t0 = a["slab"], a["tile"]
            with pe.Fori(0, KD // 2) as half:
                m = 2 * half
                for s in range(2):
                    pe.wait_ge(evac, t0 + m + s - 1)
                    for c in range(2):
                        pe.wait_ge(slab_lo, n0 + 2 * (m + s) + c + 1)
                        pe.wait_ge(a_lo_ok, hidden + KH * (c + 1))
                        products(pe, slot(s), c, 0, range(KH), a_hi, a_lo, c * KH, c == 0, c == 1).then_inc(slab_used, 1)

        L = at["load", 0]

        def load_sp(sp):
            sp.dma_start(x_tok[:, :, :], io["x_prompt"][0].rearrange("(n p) f -> p n f", p=P)).then_inc(first_in[0], 16)
            sp.dma_start(xs_tok[:, :], io["x_sample"].rearrange("b a f -> (b a) f")).then_inc(first_in[0], 16)
            for which, name in enumerate(NORMS):
                r = which * 2 * KD
                sp.dma_start(vec_rows[r:r + 2 * KD, :], io[name].rearrange("l (k p) -> (l k) p", p=P)).then_inc(first_in[1], 16)
            for c, name in enumerate(("conv_b_dw", "conv_ln_g", "conv_ln_b")):
                r = (8 + c) * KD
                sp.dma_start(vec_rows[r:r + KD, :], io[name][0].rearrange("(k p) -> k p", p=P)).then_inc(first_in[1], 16)
            sp.dma_start(tap_rows[:, :, :], io["conv_w_dw"][0].rearrange("w (k p) -> (w k) p", p=P).rearrange(
                "(a r) p -> r a p", a=2)).then_inc(first_in[1], 16)
            for j, w in ((0, io["ffn1_wg"]), (1, io["ffn1_wu"])):
                sp.dma_start(w_raw[:, j, 0:KD * P].rearrange("p (k c) -> p k c", k=KD),
                             slab_src(w[0], 0)).then_inc(slab_in[j], 16)
            for half in range(2):
                for c, name in enumerate(("attn_q_norm", "attn_k_norm")):
                    sp.dma_start(qk_gain[half * HD:(half + 1) * HD, c:c + 1],
                                 io[name].rearrange("a d -> d a")).then_inc(first_in[2], 16)
            sp.dma_start(bias[0:1, :], io["attn_logit_bias"]).then_inc(first_in[2], 16)
            sp.dma_start(pages[:, :], io["page_table"].rearrange("(a b) g -> a (b g)", a=1)).then_inc(first_in[3], 16)
            load_p(sp, 0)

        def load_p(sp, layer):
            sp.dma_start(p_tok[:, :, :], io["p_prompt"][layer, 0].rearrange("(n p) f -> p n f", p=P)).then_inc(p_in, 16)
            sp.dma_start(ps_tok[:, :], io["p_sample"][layer].rearrange("b a f -> (b a) f")).then_inc(p_in, 16)

        def load_pool(pool):
            pool.memset(ident[:, :], 0.0).then_inc(const_set, 1)
            pool.wait_ge(const_set, 1)
            pool.affine_select(out=ident[:, :], in_=ident[:, :], compare_op=ALU.not_equal, fill=1.0, base=0,
                               pattern=[[1, P]], channel_multiplier=-1).then_inc(const_ok, 1)
            for t, v in ((ones, 1.0), (from_here, 0.0), (not_before, 0.0), (head_ones, 0.0)):
                pool.memset(t[:, :], v).then_inc(const_set, 1)
            pool.memset(eps[:, 0:1], EPS).then_inc(const_set, 1)
            pool.memset(eps[:, 1:2], LN_EPS).then_inc(const_set, 1)
            pool.wait_ge(const_set, 7)
            for t, fill in ((from_here, 1.0), (not_before, -1e30)):
                pool.affine_select(out=t[:, :], in_=t[:, :], compare_op=ALU.is_gt, fill=fill, base=0,
                                   pattern=[[1, P]], channel_multiplier=-1).then_inc(const_ok, 1)
            for n, r in enumerate((0, HD)):
                pool.wait_ge(const_ok, 3 + n)
                pool.memset(head_ones[r:r + HD, r:r + HD], 1.0).then_inc(const_ok, 1)
            pool.wait_ge(const_ok, 5)

        def load_pe(pe):
            pe.wait_ge(const_ok, 1)
            pe.wait_ge(first_in[0], 32)

            def turned(m):
                if m >= 2:
                    pe.wait_ge(evac, m - 1)
                for n in range(NT):
                    pe.transpose(ps[:, m % 2, 0, n * P:(n + 1) * P], x_tok[:, n, m * P:(m + 1) * P], ident[:, :])
                pe.transpose(ps[:, m % 2, 1, 0:NS], xs_tok[:, m * P:(m + 1) * P], ident[0:NS, 0:NS]).then_inc(load_t, 1)

            turned(0)
            turned(1)
            pe.wait_ge(first_in[1], 16 * 8)
            pe.transpose(ps[:, 2, 0, 0:VECS], vec_rows[:, :], ident[0:VECS, 0:VECS])
            R = TAPS * KD // 2
            for c in range(2):
                ins = pe.transpose(ps[:, 2, 0, VECS + c * R:VECS + (c + 1) * R], tap_rows[:, c, :], ident[0:R, 0:R])
            ins.then_inc(vec_t, 1)
            for m in range(2, KD):
                turned(m)
            pe.wait_ge(const_ok, 5)
            pe.wait_ge(first_in[2], 16 * 5)
            pe.matmul(ps[:, 2, 1, 0:NH], ones[0:1, :], bias[0:1, :], start=True, stop=True).then_inc(vec_t, 1)

        def load_dve(dve):
            def x_in(m):
                dve.wait_ge(load_t, m + 1)
                dve.tensor_copy(x[:, m, 0:TP], ps[:, m % 2, 0, :])
                dve.tensor_copy(x[:, m, TP:T], ps[:, m % 2, 1, 0:NS]).then_inc(evac, 1)

            x_in(0)
            dve.wait_ge(vec_t, 1)
            dve.tensor_copy(gains[:, :], ps[:, 2, 0, 0:VECS]).then_inc(vec_ok, 1)
            dve.tensor_copy(taps[:, :], ps[:, 2, 0, VECS:VECS + TAPS * KD]).then_inc(vec_ok, 1)
            for m in range(1, KD):
                x_in(m)
                x_post_dve(dve, L, 0, 0, m - 1)
                if m == 4:
                    split_lo(dve, 0, 0)
            dve.wait_ge(vec_t, 2)
            dve.tensor_copy(bias[:, :], ps[:, 2, 1, 0:NH]).then_inc(vec_ok, 1)
            dve.tensor_scalar(qk_gain[:, 0:1], qk_gain[:, 0:1], HD ** -0.5, None, ALU.mult).then_inc(vec_ok, 1)

        def load_act(act):
            act.preload_act_table_set(LOG_EXP)
            act.wait_ge(vec_ok, 1)
            for m in range(KD - 1):
                x_post_act(act, L, 0, 0, m, m % 2)
                if m == 3:
                    act.wait_ge(slab_in[0], 16)
                    act.activation(w_hi[:, 0, 0:D], w_raw[:, 0, 0:D], ACT.Copy).then_inc(slab_hi, 1)

        def nothing(j):
            pass

        def after_to_x(a, spt, layer, which, factor):
            def act_part(act):
                def run_(j):
                    m = KD - 2 + j
                    if spt == 1 or j == 1:
                        x_post_act(act, a, layer, which, m, m % 2)
                return run_

            def dve_evac(dve):
                def run_(j):
                    m = KD - 2 + j
                    if spt == 1 or j == 1:
                        add_to_x(dve, m % 2, a["slab"] + spt * (m + 1) - 1, m, factor)
                return run_

            def dve_lo(dve):
                def run_(j):
                    if spt == 1 or j == 1:
                        x_post_dve(dve, a, layer, which, KD - 2 + j)
                return run_
            return act_part, dve_evac, dve_lo

        def after_up(a):
            def act_part(act):
                return lambda j: (silu_act, hidden_hi_act)[j](act, a, KF - 1)

            def dve_evac(dve):
                return lambda j: scaled(dve, (s_gate, s_up)[j][:, :], 2 + j, a["slab"] + 2 * KF - 2 + j)

            def dve_lo(dve):
                return lambda j: hidden_dve(dve, a, KF - 1) if j else None
            return act_part, dve_evac, dve_lo

        def after_load():
            def act_part(act):
                def run_(j):
                    if j == 0:
                        x_post_act(act, L, 0, 0, KD - 1, 1)
                return run_
            return act_part, lambda dve: lambda j: x_post_dve(dve, L, 0, 0, KD - 1) if j == 0 else None

        M = at["mix", 0]
        k_cache_in = [sem(f"k_cache_in{g}") for g in range(PG)]
        v_cache_in = [sem(f"v_cache_in{g}") for g in range(PG)]
        q_here = sem("q_here")
        sq_qk = sem("sq_qk")
        head_mm = sem("head_mm")
        head_log = sem("head_log")
        head_r = sem("head_r")
        qk_ok = sem("qk_ok")
        diag_ok = sem("diag_ok")
        kt_mm = sem("kt_mm")
        vt_mm = sem("vt_mm")
        kt_ok = sem("kt_ok")
        vt_ok = sem("vt_ok")
        k_out = sem("k_out")
        v_out = sem("v_out")
        bc_mm = sem("bc_mm")
        bc_ok = sem("bc_ok")
        kq_ok = sem("kq_ok")
        z_mm = sem("z_mm")
        z_ok = sem("z_ok")
        abs_ok = sem("abs_ok")
        sp_ok = sem("sp_ok")
        run_ok = sem("run_ok")
        c_mm = sem("c_mm")
        t_ok = sem("t_ok")
        w_ok = sem("w_ok")
        o_mm = sem("o_mm")
        o_hi_ok = sem("o_hi_ok")
        o_lo_ok = sem("o_lo_ok")
        zs_ok = sem("zs_ok")
        ls_ok = sem("ls_ok")
        cs_mm = sem("cs_mm")
        av_ok = sem("av_ok")
        avs_ok = sem("avs_ok")
        os_mm = sem("os_mm")
        os_hi_ok = sem("os_hi_ok")
        os_lo_ok = sem("os_lo_ok")

        FIRST = (P, P, 0)
        STAGE_AT = (0, 2 * 3 * P, 4 * 3 * P)
        TILES = (((2, P, 2 * P), (3, 3 * P, 3 * P)), ((1, P, P),), ((0, 0, 0),))

        def stage(st):
            w = TP - FIRST[st]
            return a_b[:, STAGE_AT[st]:STAGE_AT[st] + 2 * w].rearrange("p (e t) -> p e t", e=2)

        def l_of(st):
            return l_b[:, st % 2, :, FIRST[st]:TP]

        def sp_of(st):
            return sp_1[:, :, :] if st == 1 else sp_a[:, :, FIRST[st]:TP]

        def qkv_src(c, hp):
            return io["attn_w_qkv"][0].rearrange("(k p) f -> p k f", p=P)[:, :, ds(c * D + hp * P, P)]

        q_at = lambda m: (s_gate, s_up)[m % 2]
        r_at = lambda m: (s_act, s_prod)[m % 2]

        def attn_sp(sp):
            n0 = M["slab"]

            def kv(hp, c):
                load_slab(sp, n0 + NP + 2 * hp + c, c, qkv_src(1 + c, hp), KD)

            def page_of(cache, dst, done, b, g):
                page = sp.value_load(pages[0:1, b * PG + g:b * PG + g + 1], min_val=0, max_val=cache.shape[1] - 1)
                rows = cache[0].rearrange("n p h d -> n p (h d)")[ds(page, 1), :, :]
                sp.dma_start(dst[:, g, :], rows.rearrange("a p f -> p (a f)")).then_inc(done[g], 16)

            def k_page(b, g):
                page_of(io["cache_k"], kc, k_cache_in, b, g)

            def v_page(b, g):
                page_of(io["cache_v"], vc, v_cache_in, b, g)

            for m in range(NP):
                load_slab(sp, n0 + m, m % 2, qkv_src(0, m), KD)
            sp.wait_ge(first_in[3], 16)
            sp.wait_ge(slab_used, n0)
            for g in range(PG):
                k_page(0, g)
            for g in range(PG):
                v_page(0, g)
            for hp in range(2):
                for c in range(2):
                    kv(hp, c)
            for hp in range(NP):
                for g in range(PG):
                    if g == PG - 1 and hp:
                        sp.wait_ge(os_mm, hp)
                        for g_ in range(PG):
                            v_page(hp, g_)
                    if hp + 1 < NP:
                        sp.wait_ge(zs_ok, 9 * hp + g + 1)
                        k_page(hp + 1, g)
                    if g < 2 and hp + 2 < NP:
                        kv(hp + 2, g)
                    elif g < 2 and hp + 2 == NP:
                        load_slab(sp, n0 + 3 * NP + g, g, slab_src(io["attn_w_o"][0], g), KD)

        def attn_pe(pe):
            n0, t0 = M["slab"], M["tile"]

            def part(n, j, s, kts, wait_k=None):
                return products(pe, slot(s), j, 0, kts, h_hi, h_lo, 0, kts[0] == 0, kts[-1] == KD - 1, wait_k)

            def whole(n, j, wait_k=None):
                pe.wait_ge(slab_lo, n + 1)
                pe.wait_ge(evac, t0 - n0 + n - 1)
                part(n, j, j, range(KD), wait_k).then_inc(slab_used, 1)

            def head_sums(m, c, s):
                pe.wait_ge(sq_qk, m + 1)
                for b in range(2):
                    ins = pe.matmul(ps[:, s, b, 0:HALF], head_ones[:, :], square[:, c, b * HALF:(b + 1) * HALF],
                                    start=True, stop=True)
                ins.then_inc(head_mm, 1)

            whole(n0, 0, lambda k: pe.wait_ge(h_lo_ok, M["xt"] - KD + k + 1))
            pe.wait_ge(evac, t0)
            stat_pe(pe, M)
            whole(n0 + 1, 1)
            head_sums(0, 0, 2)
            whole(n0 + 2, 0)
            pe.wait_ge(rms_ok, M["norm"] + 1)
            head_sums(1, 1, 3)
            whole(n0 + 3, 1)
            pe.wait_ge(head_log, 1)
            head_sums(2, 0, 2)
            with pe.Fori(2, NP // 2) as half:
                for j in range(2):
                    m = 2 * half + j
                    whole(n0 + m, j)
                    pe.wait_ge(head_log, m - 2)
                    head_sums(m - 1, 1 - j, 3 - j)

            def transposed(src, s, done):
                for n in range(NT):
                    pe.transpose(ps[:, s, 0, n * P:(n + 1) * P], src[:, n * P:(n + 1) * P], ident[:, :])
                pe.transpose(ps[0:NS, s, 1, 0:P], src[:, TP:T], ident[:, :]).then_inc(done, 1)

            def k_sums(hp):
                pe.wait_ge(head_log, NP + hp)
                head_sums(NP + hp, 0, 2)

            def k_turned(hp):
                pe.wait_ge(head_log, NP + hp + 1)
                pe.wait_ge(qk_ok, NP + hp + 1)
                transposed(k_f, 2, kt_mm)

            def v_turned(hp):
                pe.wait_ge(evac, t0 + NP + 2 * hp + 2)
                transposed(v_f, 1, vt_mm)

            def q_spread(b):
                pe.wait_ge(diag_ok, b + 1)
                for c in range(2):
                    ins = pe.matmul(ps[:, 3, c, :], ones[:, :], q_diag[:, c * TP:(c + 1) * TP], start=True, stop=True)
                ins.then_inc(bc_mm, 1)

            def pair(hp, more):
                def chunk(c):
                    s = c // 4
                    n = n0 + NP + 2 * hp + 2 + s
                    if c % 4 == 0:
                        pe.wait_ge(slab_lo, n + 1)
                        pe.wait_ge(evac, t0 + NP + 2 * hp + 1 + s)
                        if s:
                            pe.wait_ge(vt_ok, 2 * hp + 2)
                    if more:
                        ins = part(n, s, s, range(c % 4 * 2, c % 4 * 2 + 2))
                        if c % 4 == 3:
                            ins.then_inc(slab_used, 1)
                    else:
                        if c == 0:
                            pe.wait_ge(o_lo_ok, hp)
                        products(pe, slot(s), s, 0, range(c % 4 * 2, min(c % 4 * 2 + 2, KD - 1)), o_hi, o_lo, 0,
                                 c % 4 == 0, False, None, (0,))

                def scores(st):
                    if st == 0:
                        pe.wait_ge(q_here, hp + 1)
                        pe.wait_ge(kt_ok, 2 * hp + 2)
                    else:
                        pe.wait_ge(z_ok, 3 * hp + st)
                    for i, c, t in TILES[st]:
                        for hd in range(2):
                            r = slice(hd * HD, hd * HD + HD)
                            ins = pe.matmul(ps[:, 2, hd, c:c + TP - t], k_f[r, i * P:(i + 1) * P], q_f[r, t:TP],
                                            start=True, stop=True)
                    ins.then_inc(z_mm, 1)

                def later_sum(st):
                    pe.wait_ge(sp_ok, 3 * hp + st + 1)
                    if st:
                        pe.wait_ge(t_ok, 3 * hp + st)
                        pe.wait_ge(run_ok, 2 * hp + st)
                    elif not isinstance(hp, int) or hp:
                        pe.wait_ge(o_lo_ok, hp)
                        pe.wait_ge(zs_ok, 9 * hp)
                    for hd in range(2):
                        pe.matmul(ps[:, 3, hd, FIRST[st]:TP], from_here[:, :], sp_of(st)[:, hd, :],
                                  start=True, stop=False)
                        old = (None, 2 * P, P)[st]
                        if st == 0:
                            ins = pe.matmul(ps[:, 3, hd, 2 * P:3 * P], ones[:, :], sp_a[:, hd, 3 * P:TP],
                                            start=False, stop=True)
                        else:
                            ins = pe.matmul(ps[:, 3, hd, old:TP], ones[:, :], run[:, hd, old:TP],
                                            start=False, stop=True)
                    ins.then_inc(c_mm, 1)

                scores(0)
                chunk(0)
                scores(1)
                chunk(1)
                scores(2)
                later_sum(0)
                chunk(2)
                later_sum(1)
                chunk(3)
                later_sum(2)
                chunk(4)
                if not isinstance(hp, int) or hp:
                    sample_output(hp - 1, 3 * hp + 3)
                pe.wait_ge(t_ok, 3 * hp + 3)
                if more:
                    q_spread(hp + 1)
                    pe.wait_ge(z_ok, 3 * hp + 3)
                    if not isinstance(hp, int) or hp:
                        pe.wait_ge(os_lo_ok, hp)
                    k_sums(hp + 1)
                chunk(5)
                chunk(6)
                if more:
                    pe.wait_ge(bc_ok, hp + 2)
                pe.wait_ge(zs_ok, 9 * hp + 8)
                pe.matmul(ps[:, 3, 1, 0:PG * NH], from_here[:, :], sps[:, :, :].rearrange("p g c -> p (g c)"),
                          start=True, stop=False)
                pe.matmul(ps[:, 3, 1, 0:(PG - 1) * NH], ones[:, :],
                          runs[:, 0:PG - 1, :].rearrange("p g c -> p (g c)"), start=False, stop=True).then_inc(cs_mm, 1)
                chunk(7)
                if more:
                    k_turned(hp + 1)
                pe.wait_ge(w_ok, 3 * hp + 3)
                for hd in range(2):
                    for st in (2, 1, 0):
                        for i, c, t in TILES[st]:
                            c -= FIRST[st]
                            ins = pe.matmul(ps[hd * HD:(hd + 1) * HD, 3, 0, t:TP], v_tok[:, i, hd * HD:(hd + 1) * HD],
                                            stage(st)[:, hd, c:c + TP - t], start=i == 0, stop=i == 3)
                ins.then_inc(o_mm, 1)
                if more:
                    v_turned(hp + 1)

            def sample_output(b, scores_read):
                pe.wait_ge(z_ok, scores_read)
                pe.wait_ge(avs_ok, 2 * b + 2)
                for k in range(KD):
                    ins = pe.matmul(ps[:, 2, 0, k:k + 1], vc[:, 0, k * P:(k + 1) * P], ones[:, 0:1], start=True, stop=True)
                ins.then_inc(os_mm, 1)

            whole(n0 + NP, 0)
            pe.wait_ge(head_log, NP - 2)
            head_sums(NP - 1, 1, 3)
            whole(n0 + NP + 1, 1)
            k_sums(0)
            pe.wait_ge(head_log, NP)
            q_spread(0)
            k_turned(0)
            v_turned(0)
            pair(0, True)
            with pe.Fori(1, NP - 1) as hp:
                pair(hp, True)
            pair(NP - 1, False)
            sample_output(NP - 1, 3 * NP)

        def attn_out_pe(pe):
            n0, t0 = at["mixout", 0]["slab"], at["mixout", 0]["tile"]
            pe.wait_ge(o_lo_ok, NP)
            for m in range(2):
                products(pe, slot(m), m, 0, range(KD - 1, KD), o_hi, o_lo, 0, False, True, None, (0,))
            pe.wait_ge(os_lo_ok, NP)
            for m in range(2):
                products(pe, slot(m), m, 0, range(KD), o_hi, o_lo, 0, True, True, None, (1,)).then_inc(slab_used, 1)
            with pe.Fori(1, KD // 2) as half:
                for j in range(2):
                    m = 2 * half + j
                    pe.wait_ge(slab_lo, n0 + m + 1)
                    pe.wait_ge(evac, t0 + m - 1)
                    products(pe, slot(j), j, 0, range(KD), o_hi, o_lo, 0, True, True).then_inc(slab_used, 1)

        def attn_act(act, prev):
            n0, t0 = M["slab"], M["tile"]

            def squares(m, src, c, t):
                act.wait_ge(evac, t + 1)
                act.activation(square[:, c, :], src[:, :], ACT.Square).then_inc(sq_qk, 1)

            def factor(m, s, dst):
                if not isinstance(m, int) or m:
                    act.wait_ge(head_r, m)
                act.wait_ge(head_mm, m + 1)
                act.activation(halves(log_ms[:, :]), slot(s), ACT.Ln, scale=1.0 / HD, bias=eps[:, 0:1]).then_inc(head_log, 1)
                act.wait_ge(head_log, m + 1)
                act.activation(dst[:, :], log_ms[:, :], ACT.Exp, scale=-0.5).then_inc(head_r, 1)

            def q_step(m, half, j):
                split_hi(act, n0 + m, n0 // 2 + half, j)
                squares(m - 2, q_at(j), j, t0 + m - 2)
                if not isinstance(m, int) or m > 2:
                    if not isinstance(m, int) or m > 4:
                        act.wait_ge(qk_ok, m - 4)
                    factor(m - 3, 3 - j, r_at(1 - j))

            for j in range(2):
                split_hi(act, n0 + j, n0 // 2, j)
                prev(j)
            stat_act(act, M)
            for m in range(2, 6):
                q_step(m, m // 2, m % 2)
            with act.Fori(3, NP // 2 + 1) as half:
                for j in range(2):
                    q_step(2 * half + j, half, j)
            act.wait_ge(qk_ok, NP - 2)
            factor(NP - 1, 3, s_prod)

            def k_squares(hp):
                squares(NP + hp, k_raw, 0, t0 + NP + 2 * hp)

            def k_factor(hp):
                act.wait_ge(qk_ok, NP + hp)
                if not isinstance(hp, int) or hp:
                    act.wait_ge(k_out, 32 * hp)
                factor(NP + hp, 2, qk_r)

            def q_copied(b):
                act.wait_ge(bc_mm, b + 1)
                if not isinstance(b, int) or b:
                    act.wait_ge(c_mm, 3 * b)
                act.activation(q_bc.rearrange("p (b t) -> p b t", b=2), ps[:, 3, :, :], ACT.Copy).then_inc(bc_ok, 1)

            def tokens(hp, c):
                dst, mm, ok, out, name = ((k_tok, kt_mm, kt_ok, k_out, "new_k"), (v_tok, vt_mm, vt_ok, v_out, "new_v"))[c]
                if not isinstance(hp, int) or hp:
                    act.wait_ge(out, 32 * hp)
                act.wait_ge(mm, hp + 1)
                act.activation(dst[:, :, :].rearrange("p n f -> p (n f)"), flat(2 - c), ACT.Copy).then_inc(ok, 1)
                act.activation(kvs_tok[:, c, :], ps[0:NS, 2 - c, 1, 0:P], ACT.Copy).then_inc(ok, 1)
                act.wait_ge(ok, 2 * hp + 2)
                act.dma_start(io[name + "_prompt"][0, 0].rearrange("(n p) h d -> p n (h d)", p=P)[:, :, ds(hp * P, P)],
                              dst[:, :, :]).then_inc(out, 16)
                act.dma_start(io[name + "_sample"][0].rearrange("b a h d -> b (a h d)")[:, ds(hp * P, P)],
                              kvs_tok[:, c, :]).then_inc(out, 16)

            def pair(hp, more):
                def softplus(st):
                    n = 3 * hp + st
                    lb = l_of(st)
                    act.wait_ge(z_ok, n + 1)
                    if st != 1 and (not isinstance(n, int) or n):
                        act.wait_ge(sp_ok, n - (st == 2))
                    act.activation(lb, stage(st), ACT.Abs).then_inc(abs_ok, 1)
                    act.wait_ge(abs_ok, 3 * n + 1)
                    act.activation(lb, lb, ACT.Exp, scale=-1.0).then_inc(abs_ok, 1)
                    act.wait_ge(abs_ok, 3 * n + 2)
                    act.activation(lb, lb, ACT.Ln, bias=1.0).then_inc(abs_ok, 1)

                def weight(st):
                    act.wait_ge(t_ok, 3 * hp + st + 1)
                    act.activation(stage(st), stage(st), ACT.Exp).then_inc(w_ok, 1)

                softplus(0)
                softplus(1)
                softplus(2)
                weight(0)
                if not isinstance(hp, int) or hp:
                    sample_hi(hp - 1)
                if more:
                    k_squares(hp + 1)
                weight(1)
                act.wait_ge(zs_ok, 9 * hp + 5)
                act.activation(ls[:, :, :], zs[:, :, :], ACT.Abs).then_inc(ls_ok, 1)
                act.wait_ge(ls_ok, 4 * hp + 1)
                act.activation(ls[:, :, :], ls[:, :, :], ACT.Exp, scale=-1.0).then_inc(ls_ok, 1)
                act.wait_ge(ls_ok, 4 * hp + 2)
                act.activation(ls[:, :, :], ls[:, :, :], ACT.Ln, bias=1.0).then_inc(ls_ok, 1)
                weight(2)
                if more:
                    split_hi(act, n0 + NP + 2 * hp + 4, (n0 + NP) // 2 + hp + 2, 0)
                if more:
                    q_copied(hp + 1)
                    k_factor(hp + 1)
                act.wait_ge(zs_ok, 9 * hp + 9)
                act.activation(ls[:, :, :], zs[:, :, :], ACT.Exp).then_inc(ls_ok, 1)
                if more:
                    tokens(hp + 1, 0)
                act.wait_ge(o_mm, hp + 1)
                act.activation(o_hi[:, ds(hp, 1), 0:TP].rearrange("p a t -> p (a t)"), flat(3), ACT.Copy).then_inc(o_hi_ok, 1)
                if more:
                    tokens(hp + 1, 1)
                    split_hi(act, n0 + NP + 2 * hp + 5, (n0 + NP) // 2 + hp + 2, 1)

            def sample_hi(b):
                act.wait_ge(os_mm, b + 1)
                act.activation(sample_at(o_hi, b), ps[:, 2, 0, 0:KD], ACT.Copy).then_inc(os_hi_ok, 1)

            k_squares(0)
            q_copied(0)
            k_factor(0)
            tokens(0, 0)
            split_hi(act, n0 + NP + 2, (n0 + NP) // 2 + 1, 0)
            tokens(0, 1)
            split_hi(act, n0 + NP + 3, (n0 + NP) // 2 + 1, 1)
            pair(0, True)
            with act.Fori(1, NP - 1) as hp:
                pair(hp, True)
            pair(NP - 1, False)
            sample_hi(NP - 1)

        def sample_at(o, b):
            return o[:, :, ds(TP + b, 1)].rearrange("p k a -> p (k a)")

        def attn_dve(dve, prev_evac, prev_lo):
            n0, t0 = M["slab"], M["tile"]

            def normed(m, dst, src, factor, c):
                dve.wait_ge(head_r, m + 1)
                dve.scalar_tensor_tensor(dst, src[:, :], qk_gain[:, c:c + 1], factor[:, :],
                                         ALU.mult, ALU.mult).then_inc(qk_ok, 1)

            def q_normed(m, j):
                dve.wait_ge(evac, t0 + m + 1)
                normed(m, q_all[:, ds(m, 1), :].rearrange("p a t -> p (a t)"), q_at(j), r_at(j), 0)

            def q_step(m, j):
                if not isinstance(m, int) or m > 4:
                    dve.wait_ge(qk_ok, m - 3)
                elif m == 4:
                    dve.wait_ge(qk_ok, 1)
                scaled(dve, q_at(j)[:, :], j, n0 + m - 2)
                split_lo(dve, n0 + m, j)
                if not isinstance(m, int) or m > 2:
                    q_normed(m - 3, 1 - j)

            for j in range(2):
                prev_evac(j)
                split_lo(dve, n0 + j, j)
                prev_lo(j)
            dve.wait_ge(rms_ok, M["norm"] + 1)
            for m in range(2, 6):
                q_step(m, m % 2)
            with dve.Fori(3, NP // 2 + 1) as half:
                for j in range(2):
                    q_step(2 * half + j, j)
            q_normed(NP - 1, 1)

            def k_evac(hp):
                dve.wait_ge(qk_ok, NP + hp)
                scaled(dve, k_raw[:, :], 0, n0 + NP + 2 * hp)

            def v_evac(hp):
                if not isinstance(hp, int) or hp:
                    dve.wait_ge(vt_mm, hp)
                scaled(dve, v_f[:, :], 1, n0 + NP + 2 * hp + 1)

            def diagonal(b):
                dve.tensor_tensor(q_diag.rearrange("p (k f) -> p k f", k=KD),
                                  ident[:, :].unsqueeze(1).broadcast_to([P, KD, P]),
                                  q_all[:, :, ds(TP + b, 1)].broadcast_to([P, KD, P]), ALU.mult).then_inc(diag_ok, 1)

            def ready(hp):
                dve.wait_ge(evac, t0 + NP + 2 * hp + 1)
                normed(NP + hp, k_f[:, :], k_raw, qk_r, 1)
                dve.tensor_copy(q_f[:, 0:TP], q_all[:, ds(hp, 1), 0:TP].rearrange("p a t -> p (a t)")).then_inc(q_here, 1)

            def pair(hp, more):
                def biased(st):
                    if st == 0 and (not isinstance(hp, int) or hp):
                        dve.wait_ge(o_mm, hp)
                    dve.wait_ge(z_mm, 3 * hp + st + 1)
                    for hd in range(2):
                        b = bias[:, ds(2 * hp + hd, 1)]
                        for i, c, t in TILES[st]:
                            c1 = c + TP - t
                            out, z = stage(st)[:, hd, c - FIRST[st]:c1 - FIRST[st]], ps[:, 2, hd, c:c1]
                            ins = dve.scalar_tensor_tensor(out[:, 0:P], z[:, 0:P], b, not_before[:, :], ALU.add, ALU.add)
                            if i < 3:
                                ins = dve.tensor_scalar(out[:, P:], z[:, P:], b, None, ALU.add)
                    ins.then_inc(z_ok, 1)

                def softplus(st):
                    n = 3 * hp + st
                    dve.wait_ge(abs_ok, 3 * n + 3)
                    dve.wait_ge(z_ok, n + 1)
                    if st == 2:
                        dve.wait_ge(run_ok, 2 * hp + 1)
                        dve.wait_ge(c_mm, 3 * hp + 1)
                    dve.scalar_tensor_tensor(sp_of(st), stage(st), 0.0, l_of(st),
                                             ALU.max, ALU.add).then_inc(sp_ok, 1)

                def running_sum(st):
                    dve.wait_ge(sp_ok, 3 * hp + st + 1)
                    if st == 0:
                        dve.wait_ge(kq_ok, PG * hp + PG)
                        dve.tensor_tensor(run[:, :, 3 * P:TP], sp_a[:, :, 2 * P:3 * P], sp_a[:, :, 3 * P:TP], ALU.add)
                        dve.tensor_copy(run[:, :, 2 * P:3 * P], sp_a[:, :, P:2 * P]).then_inc(run_ok, 1)
                    else:
                        dve.wait_ge(c_mm, 3 * hp + 2)
                        dve.wait_ge(run_ok, 2 * hp + 1)
                        dve.tensor_tensor(run[:, :, 2 * P:TP], run[:, :, 2 * P:TP], sp_1[:, :, P:], ALU.add)
                        dve.tensor_copy(run[:, :, P:2 * P], sp_1[:, :, 0:P]).then_inc(run_ok, 1)

                def log_weight(st):
                    dve.wait_ge(c_mm, 3 * hp + st + 1)
                    dve.tensor_tensor(stage(st), stage(st), ps[:, 3, :, FIRST[st]:TP], ALU.subtract).then_inc(t_ok, 1)

                def page_scores(g):
                    dve.wait_ge(kq_ok, 4 * hp + g + 1)
                    dve.tensor_reduce(zs[:, g, :], kc[:, g, :].rearrange("p (h d) -> p h d", d=HD),
                                      AX.X, ALU.add).then_inc(zs_ok, 1)

                biased(0)
                split_lo(dve, n0 + NP + 2 * hp + 3, 1)
                page_scores(0)
                biased(1)
                softplus(0)
                page_scores(1)
                softplus(1)
                biased(2)
                log_weight(0)
                running_sum(0)
                page_scores(2)
                softplus(2)
                log_weight(1)
                running_sum(1)
                if not isinstance(hp, int) or hp:
                    pages_summed(hp - 1)
                if more:
                    diagonal(hp + 1)
                if more:
                    k_evac(hp + 1)
                page_scores(3)
                dve.wait_ge(zs_ok, 9 * hp + 4)
                dve.tensor_tensor(zs[:, :, :], zs[:, :, :], bias[:, :].unsqueeze(1).broadcast_to([P, PG, NH]),
                                  ALU.add).then_inc(zs_ok, 1)
                log_weight(2)
                if not isinstance(hp, int) or hp:
                    sample_lo(hp - 1)
                dve.wait_ge(ls_ok, 4 * hp + 3)
                dve.scalar_tensor_tensor(sps[:, :, :], zs[:, :, :], 0.0, ls[:, :, :], ALU.max, ALU.add).then_inc(zs_ok, 1)
                dve.wait_ge(zs_ok, 9 * hp + 6)
                dve.tensor_tensor(runs[:, 1, :], sps[:, 2, :], sps[:, 3, :], ALU.add).then_inc(zs_ok, 1)
                dve.tensor_copy(runs[:, 2, :], sps[:, 3, :])
                dve.wait_ge(zs_ok, 9 * hp + 7)
                dve.tensor_tensor(runs[:, 0, :], runs[:, 1, :], sps[:, 1, :], ALU.add).then_inc(zs_ok, 1)
                if more:
                    split_lo(dve, n0 + NP + 2 * hp + 4, 0)
                if more:
                    ready(hp + 1)
                dve.wait_ge(cs_mm, hp + 1)
                dve.tensor_tensor(zs[:, :, :].rearrange("p g c -> p (g c)"), zs[:, :, :].rearrange("p g c -> p (g c)"),
                                  ps[:, 3, 1, 0:PG * NH], ALU.subtract).then_inc(zs_ok, 1)
                if more:
                    v_evac(hp + 1)
                dve.wait_ge(o_hi_ok, hp + 1)
                dve.tensor_tensor(o_lo[:, ds(hp, 1), 0:TP].rearrange("p a t -> p (a t)"), flat(3),
                                  o_hi[:, ds(hp, 1), 0:TP].rearrange("p a t -> p (a t)").bitcast(F32), ALU.subtract).then_inc(o_lo_ok, 1)

            def pages_summed(b):
                dve.wait_ge(av_ok, PG * b + PG)
                dve.tensor_tensor(vc[:, 0:2, :], vc[:, 0:2, :], vc[:, 2:4, :], ALU.add).then_inc(avs_ok, 1)
                dve.wait_ge(avs_ok, 2 * b + 1)
                dve.tensor_tensor(vc[:, 0, :], vc[:, 0, :], vc[:, 1, :], ALU.add).then_inc(avs_ok, 1)

            def sample_lo(b):
                dve.wait_ge(os_hi_ok, b + 1)
                dve.tensor_tensor(sample_at(o_lo, b), ps[:, 2, 0, 0:KD], sample_at(o_hi, b).bitcast(F32),
                                  ALU.subtract).then_inc(os_lo_ok, 1)

            k_evac(0)
            diagonal(0)
            v_evac(0)
            ready(0)
            split_lo(dve, n0 + NP + 2, 0)
            pair(0, True)
            with dve.Fori(1, NP - 1) as hp:
                pair(hp, True)
            pair(NP - 1, False)
            pages_summed(NP - 1)
            sample_lo(NP - 1)

        def attn_pool(pool):
            def keys(b):
                pool.wait_ge(bc_ok, b + 1)
                for g in range(PG):
                    pool.wait_ge(k_cache_in[g], 16 * b + 16)
                    pool.tensor_tensor(kc[:, g, :], kc[:, g, :], q_bc, ALU.mult).then_inc(kq_ok, 1)

            def values(b):
                pool.wait_ge(ls_ok, 4 * b + 4)
                for g in range(PG):
                    pool.wait_ge(v_cache_in[g], 16 * b + 16)
                    v = vc[:, g, :].rearrange("p (h d) -> p h d", d=HD)
                    pool.tensor_tensor(v, v, ls[:, g, :].unsqueeze(2).broadcast_to([P, NH, HD]), ALU.mult).then_inc(av_ok, 1)

            keys(0)
            with pool.Fori(1, NP) as hp:
                keys(hp)
                values(hp - 1)
            values(NP - 1)

        C = at["mix", 1]
        state_in = sem("state_in")
        state_mm = sem("state_mm")
        state_ok = sem("state_ok")
        g_ok = sem("g_ok")
        tap_prod = sem("tap_prod")
        tap_diag = sem("tap_diag")
        diag_mm = sem("diag_mm")
        tap_add = sem("tap_add")
        tap_ok = sem("tap_ok")
        y_ok = sem("y_ok")
        yp_ok = sem("yp_ok")
        yk_ok = sem("yk_ok")
        st_prod = sem("st_prod")
        ys_ok = sem("ys_ok")
        ln_mm = sem("ln_mm")
        yc_ok = sem("yc_ok")
        ysq_ok = sem("ysq_ok")
        var_ok = sem("var_ok")
        yn_ok = sem("yn_ok")
        c_fn = sem("c_fn")
        c_hi_ok = sem("c_hi_ok")
        c_lo_ok = sem("c_lo_ok")
        tail_mm = sem("tail_mm")
        tail_ok = sem("tail_ok")
        conv_out = sem("conv_out")
        early_mm = sem("early_mm")

        def share(k):
            last = isinstance(k, int) and k == KD - 1
            return (LAST_DVE, LAST_ACT, LAST_PE) if last else (TAPS_DVE, TAPS_ACT, TAPS_PE)

        def conv_sp(sp):
            n0 = C["slab"]

            def both(k):
                for c in range(2):
                    src = io["conv_w_in"][0].rearrange("(k p) f -> p k f", p=P)[:, :, ds(c * D + k * P, P)]
                    load_slab(sp, n0 + 2 * k + c, c, src, KD)
            both(0)
            both(1)
            sp.wait_ge(slab_used, n0)
            sp.dma_start(st_rows[:, :, :], io["state_conv"][0].rearrange("(a b) w f -> a (b w) f", a=2).rearrange(
                "a r f -> r a f")).then_inc(state_in, 16)
            both(2)
            sp.wait_ge(state_in, 16)
            for b in range(NS // 2):
                rows = st_rows[b * PAD + 1:(b + 1) * PAD, :, :]
                out = io["new_conv_sample"][0].rearrange("(a b) w f -> b w a f", a=2)
                sp.dma_start(out[b, 0:PAD - 1, :, :], rows).then_inc(conv_out, 16)
                both(b + 3)
            both(KD - 1)

        def conv_tail_sp(sp):
            sp.wait_ge(tail_ok, 1)
            sp.dma_start(io["new_conv_prompt"][0, 0], cv_tok[0:PAD, :]).then_inc(conv_out, 16)
            sp.dma_start(io["new_conv_sample"][0, :, PAD - 1, :], cv_tok[PAD:, :]).then_inc(conv_out, 16)

        def conv_pe(pe):
            n0, t0 = C["slab"], C["tile"]

            def tile(k, c, wait_h=False, parity=None):
                pe.wait_ge(slab_lo, n0 + 2 * k + c + 1)
                pe.wait_ge(evac, t0 + 2 * k + c - 1)
                wait_k = (lambda k: pe.wait_ge(h_lo_ok, C["xt"] - KD + k + 1)) if wait_h else None
                for part in range(2):
                    kts = range(part * KD // 2, (part + 1) * KD // 2)
                    ins = products(pe, slot(c), c, 0, kts, h_hi, h_lo, 0, part == 0, part == 1, wait_k)
                    if part == 0 and c == 0 and (not isinstance(k, int) or k > 1):
                        taps_pe(k - 1, parity)
                ins.then_inc(slab_used, 1)

            def taps_pe(k, j):
                nd, na, n = share(k)
                pe.wait_ge(g_ok, 3 * k + 2)
                pe.wait_ge(tap_diag, TAPS_PE * k + n)
                if isinstance(k, int) and k == 0:
                    pe.wait_ge(state_ok, 3)
                else:
                    pe.wait_ge(tap_ok, TAPS_DVE * (k - 1) + 2)
                for i in range(n):
                    w = nd + na + i
                    ins = pe.matmul(ps[:, 3, 0, :], (diag0, diag1)[j][:, i, :], g_pad[:, j, w:w + TP],
                                    start=i == 0, stop=i == n - 1)
                ins.then_inc(diag_mm, 1)

            tile(0, 0, True)
            pe.wait_ge(evac, t0)
            stat_pe(pe, C)
            tile(0, 1)
            tile(1, 0)
            pe.wait_ge(state_in, 16)
            R = 4 * PAD
            for s in range(2):
                if s:
                    pe.wait_ge(rms_ok, C["norm"] + 1)
                for k in range(s * 4, s * 4 + 4):
                    for a in range(2):
                        ins = pe.transpose(ps[:, 2 + s, k // 2 % 2, (k % 2) * 2 * R + a * R:(k % 2) * 2 * R + (a + 1) * R],
                                           st_rows[:, a, k * P:(k + 1) * P], ident[0:R, 0:R])
                ins.then_inc(state_mm, 1)
            taps_pe(0, 0)
            tile(1, 1)
            tile(2, 0, parity=1)
            tile(2, 1)

            def ln_sum(k):
                pe.wait_ge(yk_ok, k + 1)
                for b in range(2):
                    ins = pe.matmul(slot(2)[:, b, :], ones[:, :], y[:, ds(k, 1), b * HALF:(b + 1) * HALF].rearrange(
                        "p a t -> p (a t)"), start=isinstance(k, int) and k == 0, stop=isinstance(k, int) and k == KD - 1)
                return ins

            tile(3, 0, parity=0)
            ln_sum(0)
            tile(3, 1)
            with pe.Fori(2, KD // 2) as half:
                for j in range(2):
                    k = 2 * half + j
                    tile(k, 0, parity=1 - j)
                    ln_sum(k - 3)
                    tile(k, 1)
            ln_sum(KD - 3)
            taps_pe(KD - 1, 1)
            pe.wait_ge(g_ok, 3 * KD)
            pe.wait_ge(evac, t0 + 2 * KD)
            for k in range(KD):
                ins = pe.transpose(ps[0:PAD + NS, 0, k // 4, k % 4 * P:(k % 4 + 1) * P], g_last[:, k, :], ident[:, :])
            ins.then_inc(tail_mm, 1)
            ln_sum(KD - 2)
            ln_sum(KD - 1).then_inc(ln_mm, 1)
            for k in range(KD):
                pe.wait_ge(ysq_ok, k + 1)
                for b in range(2):
                    ins = pe.matmul(slot(1)[:, b, :], ones[:, :], square[:, k % 2, b * HALF:(b + 1) * HALF],
                                    start=k == 0, stop=k == KD - 1)
                ins.then_inc(ln_mm, 1)

        CO = at["mixout", 1]

        def conv_out_sp(sp):
            w = io["conv_w_out"][0]
            for s in range(4):
                sp.wait_ge(slab_lo, CO["slab"] + s - 1)
                sp.dma_start(w_raw[:, s % 2, 0:D].rearrange("p (k c) -> p k c", k=2),
                             w.rearrange("(k p) f -> p k f", p=P)[:, 2 * s:2 * s + 2, 0:4 * P]).then_inc(slab_in[s % 2], 16)
            for m in range(4, KD):
                load_slab(sp, CO["slab"] + m, m % 2, slab_src(w, m), KD)

        def conv_out_pe(pe):
            n0, t0 = CO["slab"], CO["tile"]
            pe.wait_ge(tail_ok, 1)

            def add(s, kk, m):
                return products(pe, slot(m), s % 2, (kk * 4 + m) * P, range(1), c_hi, c_lo, 2 * s + kk,
                                s == 0 and kk == 0, s == 3 and kk == 1)

            for s in range(3):
                pe.wait_ge(slab_lo, n0 + s + 1)
                for kk in range(2):
                    pe.wait_ge(c_lo_ok, 2 * s + kk + 1)
                    for m in range(4):
                        ins = add(s, kk, m)
                ins.then_inc(slab_used, 1)
            pe.wait_ge(slab_lo, n0 + 4)
            pe.wait_ge(c_lo_ok, KD)
            for m in range(4):
                for kk in range(2):
                    ins = add(3, kk, m)
                ins.then_inc(early_mm if m < 3 else slab_used, 1)
            for m in range(4, KD):
                pe.wait_ge(slab_lo, n0 + m + 1)
                pe.wait_ge(evac, t0 + (m - 3 if m < 6 else m - 1))
                products(pe, slot(m % 2), m % 2, 0, range(KD), c_hi, c_lo, 0, True, True).then_inc(slab_used, 1)

        def conv_out_act(act):
            n0 = CO["slab"]

            def post(m):
                x_post_act(act, CO, 1, 2, m, m % 2)

            for m in range(2, 5):
                split_hi(act, n0 + m, (n0 + m) // 2, m % 2)
            post(0)
            post(1)
            split_hi(act, n0 + 5, (n0 + 5) // 2, 1)
            post(2)
            post(3)
            for m in range(6, KD):
                split_hi(act, n0 + m, (n0 + m) // 2, m % 2)
                post(m - 2)

        def conv_out_dve(dve):
            n0 = CO["slab"]

            def add(m):
                if m < 3:
                    dve.wait_ge(early_mm, m + 1)
                else:
                    dve.wait_ge(slab_used, n0 + m + 1)
                s = m if m < 4 else m % 2
                xm = halves(x[:, m, :])
                dve.tensor_tensor(xm, slot(s), xm, ALU.add).then_inc(evac, 1)

            for m in range(2, 5):
                split_lo(dve, n0 + m, m % 2)
            add(0)
            add(1)
            x_post_dve(dve, CO, 1, 2, 0)
            add(2)
            x_post_dve(dve, CO, 1, 2, 1)
            add(3)
            split_lo(dve, n0 + 5, 1)
            x_post_dve(dve, CO, 1, 2, 2)
            x_post_dve(dve, CO, 1, 2, 3)
            for m in range(6, KD):
                split_lo(dve, n0 + m, m % 2)
                add(m - 2)
                x_post_dve(dve, CO, 1, 2, m - 2)

        def conv_act(act, prev):
            n0 = C["slab"]
            for j in range(2):
                split_hi(act, n0 + j, n0 // 2, j)
                prev(j)

            def sigmoid(k):
                act.wait_ge(evac, C["tile"] + 2 * k + 2)
                act.activation(s_act[:, :], s_gate[:, :], ACT.Sigmoid).then_inc(act_fn, 1)

            for j in range(2):
                split_hi(act, n0 + 2 + j, n0 // 2 + 1, j)
                if j == 0:
                    stat_act(act, C)
            def tap_products(k, j, part):
                nd, na, _ = share(k)
                act.wait_ge(g_ok, 3 * k + 2)
                for c in range(part * na // 2, (part + 1) * na // 2):
                    if c >= RING:
                        act.wait_ge(tap_add, (TAPS_ACT - 1) * k + max(c - RING, 1))
                    elif not isinstance(k, int) or k:
                        act.wait_ge(tap_add, (TAPS_ACT - 1) * k + c + 1 - RING)
                    w = nd + c
                    act.activation(tap_prods[:, (TAPS_ACT * j + c) % RING, :], g_pad[:, j, w:w + TP], ACT.Copy,
                                   scale=tap_now[:, j, w:w + 1]).then_inc(tap_prod, 1)

            def diagonals(k, j):
                nd, na, n = share(k)
                act.wait_ge(g_ok, 3 * k + 1)
                if not isinstance(k, int) or k > 1:
                    act.wait_ge(diag_mm, k - 1)
                for i in range(n):
                    w = nd + na + i
                    act.activation((diag0, diag1)[j][:, i, :], ident[:, :], ACT.Copy,
                                   scale=tap_now[:, j, w:w + 1]).then_inc(tap_diag, 1)

            def step(k, j, more):
                if more:
                    split_hi(act, n0 + 2 * k + 2, n0 // 2 + k + 1, 0)
                tap_products(k - 1, 1 - j, 0)
                if more:
                    split_hi(act, n0 + 2 * k + 3, n0 // 2 + k + 1, 1)
                sigmoid(k)
                diagonals(k, j)
                tap_products(k - 1, 1 - j, 1)

            sigmoid(0)
            diagonals(0, 0)
            step(1, 1, True)
            with act.Fori(1, KD // 2 - 1) as half:
                for j in range(2):
                    step(2 * half + j, j, True)
            step(KD - 2, 0, True)
            step(KD - 1, 1, False)
            for part in range(2):
                tap_products(KD - 1, 1, part)
            for j in range(2):
                split_hi(act, CO["slab"] + j, CO["slab"] // 2, j)
            for k in range(KD):
                act.wait_ge(yc_ok, k + 1)
                if k >= 2:
                    act.wait_ge(ln_mm, k)
                act.activation(square[:, k % 2, :], y[:, k, :], ACT.Square).then_inc(ysq_ok, 1)
            act.wait_ge(tail_mm, 1)
            act.activation(cv_tok[:, :], ps[0:PAD + NS, 0, :, :].rearrange("p b t -> p (b t)"), ACT.Copy).then_inc(tail_ok, 1)
            act.preload_act_table_set(LOG_EXP)
            act.wait_ge(ln_mm, KD + 1)
            act.activation(halves(s_gate[:, :]), slot(1), ACT.Ln, scale=1.0 / D, bias=eps[:, 1:2]).then_inc(var_ok, 1)
            act.wait_ge(var_ok, 1)
            act.activation(s_up[:, :], s_gate[:, :], ACT.Exp, scale=-0.5).then_inc(var_ok, 1)
            for k in range(KD):
                act.wait_ge(yn_ok, k + 1)
                act.activation(y[:, k, :], y[:, k, :], ACT.Silu, scale=gains[:, 9 * KD + k:9 * KD + k + 1],
                               bias=gains[:, 10 * KD + k:10 * KD + k + 1]).then_inc(c_fn, 1)
                act.wait_ge(c_fn, k + 1)
                act.activation(c_hi[:, k, :], y[:, k, :], ACT.Copy).then_inc(c_hi_ok, 1)

        def conv_dve(dve, prev_evac, prev_lo):
            n0, t0 = C["slab"], C["tile"]
            for j in range(2):
                prev_evac(j)
                split_lo(dve, n0 + j, j)
                prev_lo(j)
            dve.memset(g_pad[:, :, 0:PAD], 0.0).then_inc(state_ok, 1)
            dve.wait_ge(rms_ok, C["norm"] + 1)

            def state():
                for s in range(2):
                    dve.wait_ge(state_mm, s + 1)
                    for b in range(2):
                        ins = dve.tensor_copy(st[:, s * 4 + b * 2:s * 4 + b * 2 + 2, :, :],
                                              ps[:, 2 + s, b, 0:2 * NS * PAD].rearrange("p (k b w) -> p k b w", k=2, b=NS))
                    ins.then_inc(state_ok, 1)

            def state_sum():
                dve.wait_ge(st_prod, 1)
                dve.tensor_reduce(y[:, :, TP:T], st[:, :, :, :], AX.X, ALU.add).then_inc(ys_ok, 1)
                dve.wait_ge(ys_ok, 1)
                dve.tensor_tensor(y[:, :, TP:T], y[:, :, TP:T], gains[:, 8 * KD:9 * KD].unsqueeze(2).broadcast_to(
                    [P, KD, NS]), ALU.add).then_inc(ys_ok, 1)

            def taps_here(k, j):
                if not isinstance(k, int) or k > 1:
                    dve.wait_ge(tap_prod, TAPS_ACT * (k - 1))
                dve.tensor_copy(tap_now[:, j, :], taps[:, :].rearrange("p (w k) -> p k w", k=KD)[:, ds(k, 1), :].rearrange(
                    "p a w -> p (a w)")).then_inc(g_ok, 1)

            def gated(k, j):
                dve.wait_ge(act_fn, C["fn"] + k + 1)
                dve.wait_ge(evac, t0 + 2 * k + 2)
                dve.tensor_tensor(g_pad[:, j, PAD:PAD + TP], s_up[:, 0:TP], s_act[:, 0:TP], ALU.mult).then_inc(g_ok, 1)
                dve.tensor_tensor(g_last[:, ds(k, 1), :].rearrange("p a t -> p (a t)"), s_up[:, TP - PAD:T],
                                  s_act[:, TP - PAD:T], ALU.mult).then_inc(g_ok, 1)

            def own_taps(k, j, ws):
                for w in ws:
                    acc = (tap_own[:, j, :], s_prod[:, 0:TP])[w % 2]
                    src = g_pad[:, j, w:w + TP]
                    tap = tap_now[:, j, w:w + 1]
                    if w == 0:
                        if not isinstance(k, int) or k > 1:
                            dve.wait_ge(yp_ok, k - 1)
                        dve.wait_ge(g_ok, 3 * k + 2)
                        ins = dve.tensor_scalar(acc, src, tap, gains[:, ds(8 * KD + k, 1)], ALU.mult, ALU.add)
                    elif w == 1:
                        if not isinstance(k, int) or k:
                            dve.wait_ge(y_ok, k)
                        dve.wait_ge(diag_mm, k + 1)
                        ins = dve.scalar_tensor_tensor(acc, src, tap, ps[:, 3, 0, :], ALU.mult, ALU.add)
                    else:
                        dve.wait_ge(tap_ok, TAPS_DVE * k + w - 1)
                        ins = dve.scalar_tensor_tensor(acc, src, tap, acc, ALU.mult, ALU.add)
                    ins.then_inc(tap_ok, 1)

            def finish(k, j):
                yk = y[:, ds(k, 1), :].rearrange("p a t -> p (a t)")
                dve.wait_ge(tap_ok, TAPS_DVE * k + share(k)[0])
                dve.tensor_tensor(tap_own[:, j, :], tap_own[:, j, :], s_prod[:, 0:TP], ALU.add).then_inc(y_ok, 1)
                dve.wait_ge(g_ok, 3 * k + 3)
                dve.wait_ge(ys_ok, 2)
                dve.scalar_tensor_tensor(yk[:, TP:T], g_last[:, ds(k, 1), PAD:].rearrange("p a t -> p (a t)"),
                                         tap_now[:, j, PAD:TAPS], yk[:, TP:T], ALU.mult, ALU.add).then_inc(ys_ok, 1)

            def placed(k, j):
                dve.wait_ge(yp_ok, k + 1)
                dve.tensor_copy(y[:, ds(k, 1), 0:TP].rearrange("p a t -> p (a t)"), tap_sum[:, j, :]).then_inc(yk_ok, 1)

            CUT = 4

            def step(k, j, more):
                scaled(dve, s_up[:, :], 0, n0 + 2 * k)
                if more:
                    split_lo(dve, n0 + 2 * k + 2, 0)
                own_taps(k - 1, 1 - j, range(CUT))
                taps_here(k, j)
                scaled(dve, s_gate[:, :], 1, n0 + 2 * k + 1)
                if more:
                    split_lo(dve, n0 + 2 * k + 3, 1)
                gated(k, j)
                if not isinstance(k, int) or k > 1:
                    placed(k - 2, j)
                own_taps(k - 1, 1 - j, range(CUT, TAPS_DVE))
                finish(k - 1, 1 - j)

            scaled(dve, s_up[:, :], 0, n0)
            split_lo(dve, n0 + 2, 0)
            taps_here(0, 0)
            scaled(dve, s_gate[:, :], 1, n0 + 1)
            split_lo(dve, n0 + 3, 1)
            gated(0, 0)
            state()
            state_sum()
            step(1, 1, True)
            with dve.Fori(1, KD // 2 - 1) as half:
                for j in range(2):
                    step(2 * half + j, j, True)
            step(KD - 2, 0, True)
            step(KD - 1, 1, False)
            own_taps(KD - 1, 1, range(LAST_DVE))
            finish(KD - 1, 1)
            placed(KD - 2, 0)
            for j in range(2):
                split_lo(dve, CO["slab"] + j, j)
            placed(KD - 1, 1)
            for k in range(KD):
                dve.wait_ge(ln_mm, 1)
                yk = halves(y[:, k, :])
                dve.scalar_tensor_tensor(yk, slot(2), 1.0 / D, yk, ALU.mult, ALU.subtract).then_inc(yc_ok, 1)
            dve.wait_ge(var_ok, 2)
            for k in range(KD):
                dve.wait_ge(ysq_ok, k + 1)
                dve.scalar_tensor_tensor(y[:, k, :], y[:, k, :], -1.0, s_up[:, :], ALU.mult, ALU.mult).then_inc(yn_ok, 1)
                if k:
                    conv_lo(dve, k - 1)
            conv_lo(dve, KD - 1)

        def conv_lo(dve, k):
            dve.wait_ge(c_hi_ok, k + 1)
            dve.tensor_tensor(c_lo[:, k, :], y[:, k, :], c_hi[:, k, :].bitcast(F32), ALU.subtract).then_inc(c_lo_ok, 1)

        def conv_pool(pool):
            pool.wait_ge(state_ok, 3)
            pool.tensor_tensor(st[:, :, :, :], st[:, :, :, :],
                               taps[:, 0:PAD * KD].rearrange("p (w k) -> p k w", k=KD).unsqueeze(2).broadcast_to(
                                   [P, KD, NS, PAD]), ALU.mult).then_inc(st_prod, 1)

            def tile(k, j):
                ring = lambda c: tap_prods[:, (TAPS_ACT * j + c) % RING, :]
                na = share(k)[1]
                for c in range(1, na):
                    pool.wait_ge(tap_prod, TAPS_ACT * k + c + 1)
                    if c == 1:
                        if not isinstance(k, int) or k > 1:
                            pool.wait_ge(yk_ok, k - 1)
                        pool.tensor_tensor(tap_sum[:, j, :], ring(0), ring(1), ALU.add).then_inc(tap_add, 1)
                    else:
                        pool.wait_ge(tap_add, (TAPS_ACT - 1) * k + c - 1)
                        pool.tensor_tensor(tap_sum[:, j, :], tap_sum[:, j, :], ring(c), ALU.add).then_inc(tap_add, 1)
                pool.wait_ge(y_ok, k + 1)
                pool.wait_ge(tap_add, (TAPS_ACT - 1) * k + na - 1)
                pool.tensor_tensor(tap_sum[:, j, :], tap_sum[:, j, :], tap_own[:, j, :], ALU.add).then_inc(yp_ok, 1)

            tile(0, 0)
            tile(1, 1)
            with pool.Fori(1, KD // 2 - 1) as half:
                for j in range(2):
                    tile(2 * half + j, j)
            tile(KD - 2, 0)
            tile(KD - 1, 1)

        y_mm = sem("y_mm")
        y_tok = sem("y_tok")
        y_out = [sem("y_out0"), sem("y_out1")]

        def ple_sp(sp, a, layer):
            n0 = a["slab"]
            for g in range(2):
                src = io["ple_w_proj"][layer].rearrange("(k p) f -> p k f", p=P)[:, :, g * 4 * P:(g + 1) * 4 * P]
                sp.wait_ge(slab_lo, n0 + g - 1)
                sp.dma_start(w_raw[:, g, 0:KP * 4 * P].rearrange("p (k c) -> p k c", k=KP), src).then_inc(slab_in[g], 16)
            with sp.Fori(0, KD // 2) as half:
                for j in range(2):
                    load_slab(sp, n0 + 2 + 2 * half + j, j, slab_src(io["ple_w_gate"][layer], 2 * half + j), KD)
            if layer == 0:
                load_p(sp, 1)
            else:
                for m in range(KD):
                    sp.wait_ge(y_tok, 2 * m + 2)
                    sp.dma_start(io["y_prompt"][0].rearrange("(n p) f -> p n f", p=P)[:, :, m * P:(m + 1) * P],
                                 out_tok[:, m % 2, :, :]).then_inc(y_out[m % 2], 16)
                sp.dma_start(io["y_sample"].rearrange("b a f -> (b a) f"), outs_tok[:, :]).then_inc(y_out[0], 16)

        def ple_pe(pe, a, layer):
            n0, t0 = a["slab"], a["tile"]
            pe.wait_ge(p_in, 32 * (layer + 1))
            for k in range(KP):
                for n in range(NT):
                    pe.transpose(ps[:, 2 + k, 0, n * P:(n + 1) * P], p_tok[:, n, k * P:(k + 1) * P], ident[:, :])
                pe.transpose(ps[:, 2 + k, 1, 0:NS], ps_tok[:, k * P:(k + 1) * P], ident[0:NS, 0:NS]).then_inc(p_t, 1)
            for m in range(KD):
                g, q = divmod(m, 4)
                if q == 0:
                    pe.wait_ge(slab_lo, n0 + g + 1)
                if m == 0:
                    pe.wait_ge(p_lo_ok, 2 * KP * (layer + 1))
                pe.wait_ge(evac, t0 + m - 1)
                for k in range(KP):
                    w = slice((k * 4 + q) * P, (k * 4 + q + 1) * P)
                    for n, (wt, mv) in enumerate(((w_hi, p_hi), (w_hi, p_lo), (w_lo, p_hi))):
                        for b in range(2):
                            ins = pe.matmul(ps[:, m % 2, b, 0:HALF], wt[:, g, w], mv[:, k, b * HALF:(b + 1) * HALF],
                                            start=k == 0 and n == 0, stop=k == KP - 1 and n == 2)
                ins.then_inc(slab_used if q == 3 else pp_mm, 1)

            def gate(m, s, wait_h=False):
                pe.wait_ge(slab_lo, n0 + 3 + m)
                pe.wait_ge(evac, t0 + KD + m - 1)
                wait_k = (lambda k: pe.wait_ge(h_lo_ok, at["down2", layer]["xt"] + k + 1)) if wait_h else None
                products(pe, slot(s), s, 0, range(KD), h_hi, h_lo, 0, True, True, wait_k).then_inc(slab_used, 1)

            def turned(m):
                pe.wait_ge(x_new, KD + m + 1)
                pe.wait_ge(y_tok, 2 * m - 2) if m > 1 else None
                for n in range(NT):
                    pe.transpose(ps[:, 2 + m % 2, 0, n * P:(n + 1) * P], x[:, m, n * P:(n + 1) * P], ident[:, :])
                pe.transpose(ps[0:NS, 2 + m % 2, 1, 0:P], x[:, m, TP:T], ident[:, :]).then_inc(y_mm, 1)

            gate(0, 0, True)
            stat_pe(pe, dict(a, xt=at["down2", layer]["xt"] + KD))
            gate(1, 1)
            if layer == 0:
                with pe.Fori(1, KD // 2) as half:
                    gate(2 * half, 0)
                    gate(2 * half + 1, 1)
            else:
                pe.wait_ge(rms_ok, a["norm"] + 1)
                for m in range(2, KD):
                    gate(m, m % 2)
                    if m >= 4:
                        turned(m - 4)
                for m in range(4, KD):
                    turned(m)

        def ple_act(act, a, layer, prev):
            n0 = a["slab"]
            split_hi(act, n0, n0 // 2, 0)
            for k in range(KP):
                act.wait_ge(p_t, KP * layer + k + 1)
                act.activation(p_hi[:, k, 0:TP], ps[:, 2 + k, 0, :], ACT.Copy).then_inc(p_hi_ok, 1)
                act.activation(p_hi[:, k, TP:T], ps[:, 2 + k, 1, 0:NS], ACT.Copy).then_inc(p_hi_ok, 1)
            prev(0)
            split_hi(act, n0 + 1, n0 // 2, 1)
            prev(1)
            split_hi(act, n0 + 2, n0 // 2 + 1, 0)
            split_hi(act, n0 + 3, n0 // 2 + 1, 1)
            stat_act(act, a)

            def sigmoid(m):
                act.wait_ge(evac, a["tile"] + KD + m + 1)
                act.activation(s_act[:, :], s_gate[:, :], ACT.Sigmoid).then_inc(act_fn, 1)

            def finish(m):
                if layer == 0:
                    act.wait_ge(x_new, m + 1)
                    act.wait_ge(acc_ok, a["xt"] + m - 1)
                    act.activation(square[:, m % 2, :], x[:, m, :],
                                   ACT.Square).then_inc(sq_ok, 1)
                else:
                    act.wait_ge(y_mm, m + 1)
                    if m >= 2:
                        act.wait_ge(y_out[m % 2], 16 * (m // 2))
                    act.activation(out_tok[:, m % 2, :, :].rearrange("p n f -> p (n f)"), ps[:, 2 + m % 2, 0, :],
                                   ACT.Copy).then_inc(y_tok, 1)
                    act.activation(outs_tok[:, m * P:(m + 1) * P], ps[0:NS, 2 + m % 2, 1, 0:P], ACT.Copy).then_inc(y_tok, 1)

            def next_h(m):
                act.activation(h_hi[:, m, :], x[:, m, :], ACT.Copy, scale=gain_col(1, 0, m)).then_inc(h_hi_ok, 1)

            for m in range(KD):
                if m < KD - 2 or layer == 0 and m < KD - 1:
                    split_hi(act, n0 + 4 + m, n0 // 2 + 2 + m // 2, m % 2)
                if layer == 0 and m == KD - 1:
                    act.wait_ge(slab_used, n0 + 2 + KD)
                    next_h(0)
                    next_h(1)
                sigmoid(m)
                if layer == 0:
                    finish(m)
                elif m >= 4:
                    finish(m - 4)
            if layer == 0:
                for m in range(2, KD):
                    next_h(m)
                split_hi(act, n0 + 3 + KD, (n0 + 3 + KD) // 2, 1)
            if layer == 1:
                for m in range(4, KD):
                    finish(m)

        def ple_dve(dve, a, layer, prev_evac, prev_lo):
            n0, t0 = a["slab"], a["tile"]
            prev_evac(0)
            prev_evac(1)
            split_lo(dve, n0, 0)
            for k in range(KP):
                for c, (lo, hi, src) in enumerate(((p_lo[:, k, 0:TP], p_hi[:, k, 0:TP], ps[:, 2 + k, 0, :]),
                                                   (p_lo[:, k, TP:T], p_hi[:, k, TP:T], ps[:, 2 + k, 1, 0:NS]))):
                    dve.wait_ge(p_hi_ok, 2 * (KP * layer + k) + c + 1)
                    dve.tensor_tensor(lo, src, hi.bitcast(F32), ALU.subtract).then_inc(p_lo_ok, 1)
            split_lo(dve, n0 + 1, 1)
            prev_lo(0)
            prev_lo(1)
            for m in range(KD):
                g, q = divmod(m, 4)
                dve.wait_ge(slab_used, n0 + g + 1) if q == 3 else dve.wait_ge(pp_mm, 6 * layer + 3 * g + q + 1)
                dve.tensor_copy(halves(pp[:, m, :]), slot(m % 2)).then_inc(evac, 1)
                if q == 3:
                    split_lo(dve, n0 + 2 + g, g)
            dve.wait_ge(rms_ok, a["norm"] + 1)
            for m in range(KD):
                scaled(dve, s_gate[:, :], m % 2, n0 + 2 + m)
                if m < KD - 2 or layer == 0 and m < KD - 1:
                    split_lo(dve, n0 + 4 + m, m % 2)
                if layer == 0 and m == KD - 1:
                    x_post_dve(dve, a, 1, 0, 0)
                    x_post_dve(dve, a, 1, 0, 1)
                dve.wait_ge(act_fn, a["fn"] + m + 1)
                dve.tensor_tensor(s_prod[:, :], s_act[:, :], pp[:, m, :], ALU.mult).then_inc(prod_x, 1)
                dve.wait_ge(prod_x, KD * layer + m + 1)
                dve.tensor_tensor(x[:, m, :], x[:, m, :], s_prod[:, :], ALU.add).then_inc(x_new, 1)
            if layer == 0:
                for m in range(2, KD):
                    x_post_dve(dve, a, 1, 0, m)
                split_lo(dve, n0 + 3 + KD, 1)

        def ple_pool(pool, a):
            for m in range(KD):
                x_add_pool(pool, a, m, m % 2, m == 0)

        block = ctx.enter_context(nc.Block())
        LAYERS = range(2)

        @block.sync
        def _(sp):
            load_sp(sp)
            for layer in LAYERS:
                up_sp(sp, at["up1", layer], layer, io["ffn1_wg"], io["ffn1_wu"])
                to_x_sp(sp, at["down1", layer], 2, io["ffn1_wd"][layer])
                if layer == 0:
                    attn_sp(sp)
                    to_x_sp(sp, at["mixout", 0], 1, io["attn_w_o"][0], loaded=2)
                else:
                    conv_sp(sp)
                    conv_out_sp(sp)
                    conv_tail_sp(sp)
                up_sp(sp, at["up2", layer], layer, io["ffn2_wg"], io["ffn2_wu"])
                to_x_sp(sp, at["down2", layer], 2, io["ffn2_wd"][layer])
                ple_sp(sp, at["ple", layer], layer)
            sp.wait_ge(k_out, 32 * NP)
            sp.wait_ge(v_out, 32 * NP)
            sp.wait_ge(conv_out, 96)
            sp.wait_ge(y_out[0], 16 * (KD // 2 + 1))
            sp.wait_ge(y_out[1], 16 * (KD // 2))

        @block.gpsimd
        def _(pool):
            load_pool(pool)
            add_squares_pool(pool, L)
            for layer in LAYERS:
                add_squares_pool(pool, at["down1", layer])
                (attn_pool, conv_pool)[layer](pool)
                add_squares_pool(pool, at["mixout", layer])
                add_squares_pool(pool, at["down2", layer])
                if layer == 0:
                    ple_pool(pool, at["ple", 0])

        after = {}
        for layer in LAYERS:
            after["up1", layer] = after_up(at["up1", layer])
            after["up2", layer] = after_up(at["up2", layer])
            after["down1", layer] = after_to_x(at["down1", layer], 2, layer, 1, 0.5)
            after["mixout", layer] = after_to_x(at["mixout", layer], 1, layer, 2, 1.0)
            after["down2", layer] = after_to_x(at["down2", layer], 2, layer, 3, 0.5)
        load_act_part, load_lo_part = after_load()

        @block.scalar
        def _(act):
            load_act(act)
            for layer in LAYERS:
                up_act(act, at["up1", layer], load_act_part(act) if layer == 0 else None)
                to_x_act(act, at["down1", layer], 2, layer, 1, after["up1", layer][0](act))
                (attn_act, conv_act)[layer](act, after["down1", layer][0](act))
                if layer == 0:
                    act.wait_ge(k_out, 32 * NP)
                    act.wait_ge(v_out, 32 * NP)
                    to_x_act(act, at["mixout", 0], 1, 0, 2, None)
                else:
                    conv_out_act(act)
                    act.wait_ge(conv_out, 96)
                up_act(act, at["up2", layer], after["mixout", layer][0](act))
                to_x_act(act, at["down2", layer], 2, layer, 3, after["up2", layer][0](act))
                ple_act(act, at["ple", layer], layer, after["down2", layer][0](act))

        @block.vector
        def _(dve):
            load_dve(dve)
            for layer in LAYERS:
                up_dve(dve, at["up1", layer], nothing, load_lo_part(dve) if layer == 0 else None)
                to_x_dve(dve, at["down1", layer], 2, layer, 1, 0.5, after["up1", layer][1](dve), after["up1", layer][2](dve))
                (attn_dve, conv_dve)[layer](dve, after["down1", layer][1](dve), after["down1", layer][2](dve))
                if layer == 0:
                    to_x_dve(dve, at["mixout", 0], 1, 0, 2, 1.0, None, None)
                else:
                    conv_out_dve(dve)
                up_dve(dve, at["up2", layer], after["mixout", layer][1](dve), after["mixout", layer][2](dve))
                to_x_dve(dve, at["down2", layer], 2, layer, 3, 0.5, after["up2", layer][1](dve), after["up2", layer][2](dve))
                ple_dve(dve, at["ple", layer], layer, after["down2", layer][1](dve), after["down2", layer][2](dve))

        @block.tensor
        def _(pe):
            load_pe(pe)
            for layer in LAYERS:
                U1, U2 = at["up1", layer], at["up2", layer]
                up_pe(pe, U1)
                down_pe(pe, at["down1", layer], U1["hid"])
                (attn_pe, conv_pe)[layer](pe)
                if layer == 0:
                    attn_out_pe(pe)
                else:
                    conv_out_pe(pe)
                up_pe(pe, U2)
                down_pe(pe, at["down2", layer], U2["hid"])
                ple_pe(pe, at["ple", layer], layer)

_INS = ("x_prompt", "x_sample", "cache_k", "cache_v", "state_conv", "page_table", "p_prompt", "p_sample",
        "norm_ffn1", "ffn1_wg", "ffn1_wu", "ffn1_wd", "norm_mix", "attn_w_qkv", "attn_q_norm", "attn_k_norm",
        "attn_logit_bias", "attn_w_o", "conv_w_in", "conv_w_dw", "conv_b_dw", "conv_ln_g", "conv_ln_b",
        "conv_w_out", "norm_ffn2", "ffn2_wg", "ffn2_wu", "ffn2_wd", "norm_ple", "ple_w_gate", "ple_w_proj")
_OUTS = (("y_prompt", (1, 512, 1024)), ("y_sample", (8, 1, 1024)),
         ("new_k_prompt", (1, 1, 512, 16, 64)), ("new_v_prompt", (1, 1, 512, 16, 64)),
         ("new_k_sample", (1, 8, 1, 16, 64)), ("new_v_sample", (1, 8, 1, 16, 64)),
         ("new_conv_prompt", (1, 1, 30, 1024)), ("new_conv_sample", (1, 8, 30, 1024)))

def kernel(**inputs):
    import numpy as _np
    import concourse.bacc as _bacc
    from concourse import mybir as _mybir
    from concourse.bass_utils import run_bass_kernel_spmd as _run

    nc = _bacc.Bacc("TRN2", target_bir_lowering=False, num_devices=1)
    arrays, io = {}, {}
    for name in _INS:
        a = _np.ascontiguousarray(inputs[name])
        arrays[f"in_{name}"] = a
        io[name] = nc.dram_tensor(f"in_{name}", a.shape, _mybir.dt.from_np(a.dtype), kind="ExternalInput").ap()
    for name, shape in _OUTS:
        io[name] = nc.dram_tensor(f"out_{name}", shape, _mybir.dt.float32, kind="ExternalOutput").ap()
    build(nc, io)
    r = _run(nc, [arrays], core_ids=[0])
    return tuple(r.results[0][f"out_{name}"] for name, _ in _OUTS)
```
